# Optimizing a Trainium2 kernel written in Bass

```python
import math
import jax, jax.numpy as jnp
from jax import lax
import numpy as np

D_MODEL = 1024
BATCH = 1
SEQ = 256
DEPTH = 2

RMS_EPS = 1e-6
CHUNK = 128
A_HEADS = 4
A_HEAD_DIM = D_MODEL // 8
A_WIDTH = A_HEADS * A_HEAD_DIM
B_GROUP = 16
B_WIDTH = D_MODEL // 2
B_GROUPS = B_WIDTH // B_GROUP
B_STATE = 64
DT_MIN = 1e-3
DT_MAX = 1e-1
AB_IN = 2 * A_WIDTH + B_WIDTH
AB_OUT = A_WIDTH + B_WIDTH
C_HEADS = 8
QK_NOPE = 128
QK_ROPE = 64
V_HEAD = 128
Q_LORA = 384
KV_LORA = 256
C_IN = Q_LORA + KV_LORA + QK_ROPE
ROPE_THETA = 10000.0
Q_BLOCK = 128
D_FF = 2816
N_EXPERTS = 8
TOP_K = 2
D_FF_EXPERT = 3584
MOE_BLOCK = 128

kernel_name = "hybrid_sgu_s5_mla_moe_encoder"

def rmsnorm(x, g):
    xf = x.astype(jnp.float32)
    y = xf * lax.rsqrt(jnp.mean(xf * xf, axis=-1, keepdims=True) + RMS_EPS)
    return (y * g.astype(jnp.float32)).astype(x.dtype)

def modulate(h, shift, scale):
    return h * (1.0 + scale[:, None, :]) + shift[:, None, :]

def chunked_sgu(u, v, v_g, w_s, b_s):
    bn, seq = u.shape[:2]
    v = rmsnorm(v, v_g)
    vc = v.reshape(bn, seq // CHUNK, CHUNK, A_HEADS, A_HEAD_DIM)
    s = jnp.einsum('gqk,bnkgc->bnqgc', w_s, vc) + b_s.T[None, None, :, :, None]
    return u * s.reshape(u.shape)

def s5_scan(u, lam_re, lam_im, log_dt, b_re, b_im, c_re, c_im, reverse):
    f32 = jnp.float32
    lam_re, lam_im = lam_re.astype(f32), lam_im.astype(f32)
    dt = jnp.exp(log_dt.astype(f32))[:, None]
    mag = jnp.exp(lam_re * dt)
    ang = lam_im * dt
    abar_re, abar_im = mag * jnp.cos(ang), mag * jnp.sin(ang)
    den = lam_re * lam_re + lam_im * lam_im
    fr = ((abar_re - 1.0) * lam_re + abar_im * lam_im) / den
    fi = (abar_im * lam_re - (abar_re - 1.0) * lam_im) / den
    b_re, b_im = b_re.astype(f32), b_im.astype(f32)
    bb_re = fr[:, :, None] * b_re - fi[:, :, None] * b_im
    bb_im = fr[:, :, None] * b_im + fi[:, :, None] * b_re
    bu_re = jnp.einsum('gph,blgh->blgp', bb_re, u)
    bu_im = jnp.einsum('gph,blgh->blgp', bb_im, u)
    a_re = jnp.broadcast_to(abar_re, bu_re.shape)
    a_im = jnp.broadcast_to(abar_im, bu_im.shape)

    def combine(e1, e2):
        a1r, a1i, b1r, b1i = e1
        a2r, a2i, b2r, b2i = e2
        return (a2r * a1r - a2i * a1i,
                a2r * a1i + a2i * a1r,
                a2r * b1r - a2i * b1i + b2r,
                a2r * b1i + a2i * b1r + b2i)

    _, _, x_re, x_im = lax.associative_scan(combine, (a_re, a_im, bu_re, bu_im),
                                            reverse=reverse, axis=1)
    return (jnp.einsum('ghp,blgp->blgh', c_re.astype(f32), x_re)
            - jnp.einsum('ghp,blgp->blgh', c_im.astype(f32), x_im))

def s5_mixer(u, lam_re, lam_im, log_dt, b_re, b_im, c_re, c_im, d_skip, w_glu):
    bn, seq, _ = u.shape
    uf = u.astype(jnp.float32)
    ug = uf.reshape(bn, seq, B_GROUPS, B_GROUP)
    y = (s5_scan(ug, lam_re[0], lam_im[0], log_dt[0], b_re[0], b_im[0], c_re[0], c_im[0], False)
         + s5_scan(ug, lam_re[1], lam_im[1], log_dt[1], b_re[1], b_im[1], c_re[1], c_im[1], True))
    y = y.reshape(bn, seq, B_WIDTH) + d_skip.astype(jnp.float32) * uf
    y = jax.nn.gelu(y).astype(u.dtype)
    return y * jax.nn.sigmoid(y @ w_glu)

def ab_mixer(h, w_in, v_g, w_s, b_s, lam_re, lam_im, log_dt, b_re, b_im, c_re, c_im,
             d_skip, w_glu, w_out):
    bn, seq, _ = h.shape
    z = h @ w_in
    za = jax.nn.gelu(z[..., :2 * A_WIDTH])
    u_a = za[..., :A_WIDTH].reshape(bn, seq, A_HEADS, A_HEAD_DIM)
    v_a = za[..., A_WIDTH:].reshape(bn, seq, A_HEADS, A_HEAD_DIM)
    a_out = chunked_sgu(u_a, v_a, v_g, w_s, b_s).reshape(bn, seq, A_WIDTH)
    b_out = s5_mixer(z[..., 2 * A_WIDTH:], lam_re, lam_im, log_dt, b_re, b_im, c_re, c_im,
                     d_skip, w_glu)
    return jnp.concatenate([a_out, b_out], axis=-1) @ w_out

def rope(x, cos, sin):
    xf = x.astype(jnp.float32)
    half = xf.shape[-1] // 2
    x1, x2 = xf[..., :half], xf[..., half:]
    return jnp.concatenate([x1 * cos - x2 * sin, x1 * sin + x2 * cos], axis=-1).astype(x.dtype)

def mla_mixer(h, w_in, q_norm_g, kv_norm_g, w_uq, w_ukv, w_o):
    bn, seq, _ = h.shape
    z = h @ w_in
    cq = rmsnorm(z[..., :Q_LORA], q_norm_g)
    ckv = rmsnorm(z[..., Q_LORA:Q_LORA + KV_LORA], kv_norm_g)
    k_rope = z[..., Q_LORA + KV_LORA:]
    q = (cq @ w_uq).reshape(bn, seq, C_HEADS, QK_NOPE + QK_ROPE)
    kv = (ckv @ w_ukv).reshape(bn, seq, C_HEADS, QK_NOPE + V_HEAD)
    q_nope, q_rope = q[..., :QK_NOPE], q[..., QK_NOPE:]
    k_nope, v = kv[..., :QK_NOPE], kv[..., QK_NOPE:]

    pos = jnp.arange(seq, dtype=jnp.float32)
    inv_freq = ROPE_THETA ** (-jnp.arange(0, QK_ROPE, 2, dtype=jnp.float32) / QK_ROPE)
    ang = pos[:, None] * inv_freq[None, :]
    cos, sin = jnp.cos(ang), jnp.sin(ang)
    q_rope = rope(q_rope, cos[None, :, None, :], sin[None, :, None, :])
    k_rope = rope(k_rope, cos[None], sin[None])

    scale = 1.0 / math.sqrt(QK_NOPE + QK_ROPE)
    nb = seq // Q_BLOCK
    qn_b = q_nope.reshape(bn, nb, Q_BLOCK, C_HEADS, QK_NOPE).transpose(1, 0, 2, 3, 4)
    qr_b = q_rope.reshape(bn, nb, Q_BLOCK, C_HEADS, QK_ROPE).transpose(1, 0, 2, 3, 4)

    def attend(blk):
        qn, qr = blk
        s = (jnp.einsum('bqhd,bkhd->bhqk', qn, k_nope)
             + jnp.einsum('bqhr,bkr->bhqk', qr, k_rope))
        p = jax.nn.softmax(s.astype(jnp.float32) * scale, axis=-1).astype(v.dtype)
        return jnp.einsum('bhqk,bkhd->bqhd', p, v)

    o = lax.map(attend, (qn_b, qr_b))
    o = o.transpose(1, 0, 2, 3, 4).reshape(bn, seq, C_HEADS * V_HEAD)
    return o @ w_o

def swiglu(h, w1, w3, w2):
    return (jax.nn.silu(h @ w1) * (h @ w3)) @ w2

def moe_swiglu(h, w_router, w1, w3, w2):
    bn, seq, d = h.shape
    t = bn * seq
    xf = h.reshape(t, d)
    logits = (xf @ w_router).astype(jnp.float32)
    top_val, top_idx = lax.top_k(logits, TOP_K)
    gates = jax.nn.softmax(top_val, axis=-1)
    e_flat = top_idx.reshape(-1).astype(jnp.int32)
    tok_flat = jnp.repeat(jnp.arange(t, dtype=jnp.int32), TOP_K)
    g_flat = gates.reshape(-1)
    order = jnp.argsort(e_flat, stable=True)
    e_sorted = e_flat[order]
    counts = jax.ops.segment_sum(jnp.ones_like(e_flat), e_flat, num_segments=N_EXPERTS)
    padded = ((counts + MOE_BLOCK - 1) // MOE_BLOCK) * MOE_BLOCK
    pad_end = jnp.cumsum(padded)
    pad_start = pad_end - padded
    start = jnp.cumsum(counts) - counts
    dest = pad_start[e_sorted] + (jnp.arange(t * TOP_K, dtype=jnp.int32) - start[e_sorted])
    n_rows = t * TOP_K + N_EXPERTS * MOE_BLOCK
    row_tok = jnp.full((n_rows,), t, jnp.int32).at[dest].set(tok_flat[order])
    row_gate = jnp.zeros((n_rows,), jnp.float32).at[dest].set(g_flat[order])
    nb = n_rows // MOE_BLOCK
    blk_start = jnp.arange(nb, dtype=jnp.int32) * MOE_BLOCK
    blk_expert = jnp.minimum(jnp.searchsorted(pad_end, blk_start, side='right'), N_EXPERTS - 1)
    x_pad = jnp.concatenate([xf, jnp.zeros((1, d), xf.dtype)], axis=0)
    xr = x_pad[row_tok].reshape(nb, MOE_BLOCK, d)

    def expert_block(args):
        xb, e = args
        return swiglu(xb, w1[e], w3[e], w2[e])

    yr = lax.map(expert_block, (xr, blk_expert)).reshape(n_rows, d)
    yr = yr * row_gate[:, None].astype(yr.dtype)
    y = jax.ops.segment_sum(yr, row_tok, num_segments=t + 1)[:t]
    return y.reshape(bn, seq, d)

def setup_inputs(seed: int = 0) -> dict:
    key = jax.random.key(seed)
    ks = iter(jax.random.split(key, 40))
    f32 = jnp.float32
    n_even = (DEPTH + 1) // 2
    n_odd = DEPTH // 2
    D = D_MODEL

    def nrm(shape, scale):
        return jax.random.normal(next(ks), shape, f32) * scale

    x = nrm((BATCH, SEQ, D), 1.0)
    c = nrm((BATCH, D), 1.0)
    gate_offset = jnp.repeat(jnp.array([0., 0., 1., 0., 0., 1.], f32), D)
    ada_w = nrm((DEPTH, D, 6 * D), 0.02)
    ada_b = nrm((DEPTH, 6 * D), 0.02) + gate_offset[None]
    norm_mix_g = 1.0 + nrm((DEPTH, D), 0.05)
    norm_ffn_g = 1.0 + nrm((DEPTH, D), 0.05)
    final_g = 1.0 + nrm((D,), 0.05)

    ab_w_in = nrm((n_even, D, AB_IN), D ** -0.5)
    sgu_v_g = 1.0 + nrm((n_even, A_HEADS, A_HEAD_DIM), 0.05)
    sgu_w_s = nrm((n_even, A_HEADS, CHUNK, CHUNK), CHUNK ** -0.5)
    sgu_b_s = 1.0 + nrm((n_even, A_HEADS, CHUNK), 0.1)
    s5_lam_re = -0.5 + nrm((n_even, 2, B_GROUPS, B_STATE), 0.01)
    s5_lam_im = (math.pi * jnp.arange(B_STATE, dtype=f32))[None, None, None, :] \
        + nrm((n_even, 2, B_GROUPS, B_STATE), 0.01)
    s5_log_dt = jax.random.uniform(next(ks), (n_even, 2, B_GROUPS), f32,
                                   math.log(DT_MIN), math.log(DT_MAX))
    s5_b_re = nrm((n_even, 2, B_GROUPS, B_STATE, B_GROUP), (2 * B_GROUP) ** -0.5)
    s5_b_im = nrm((n_even, 2, B_GROUPS, B_STATE, B_GROUP), (2 * B_GROUP) ** -0.5)
    s5_c_re = nrm((n_even, 2, B_GROUPS, B_GROUP, B_STATE), 0.5)
    s5_c_im = nrm((n_even, 2, B_GROUPS, B_GROUP, B_STATE), 0.5)
    s5_d = nrm((n_even, B_WIDTH), 1.0)
    s5_w_glu = nrm((n_even, B_WIDTH, B_WIDTH), B_WIDTH ** -0.5)
    ab_w_out = nrm((n_even, AB_OUT, D), AB_OUT ** -0.5)

    ffn_w1 = nrm((n_even, D, D_FF), D ** -0.5)
    ffn_w3 = nrm((n_even, D, D_FF), D ** -0.5)
    ffn_w2 = nrm((n_even, D_FF, D), D_FF ** -0.5)

    mla_w_in = nrm((n_odd, D, C_IN), D ** -0.5)
    mla_q_norm_g = 1.0 + nrm((n_odd, Q_LORA), 0.05)
    mla_kv_norm_g = 1.0 + nrm((n_odd, KV_LORA), 0.05)
    mla_w_uq = nrm((n_odd, Q_LORA, C_HEADS * (QK_NOPE + QK_ROPE)), Q_LORA ** -0.5)
    mla_w_ukv = nrm((n_odd, KV_LORA, C_HEADS * (QK_NOPE + V_HEAD)), KV_LORA ** -0.5)
    mla_w_o = nrm((n_odd, C_HEADS * V_HEAD, D), (C_HEADS * V_HEAD) ** -0.5)

    moe_w_router = nrm((n_odd, D, N_EXPERTS), D ** -0.5)
    moe_w1 = nrm((n_odd, N_EXPERTS, D, D_FF_EXPERT), D ** -0.5)
    moe_w3 = nrm((n_odd, N_EXPERTS, D, D_FF_EXPERT), D ** -0.5)
    moe_w2 = nrm((n_odd, N_EXPERTS, D_FF_EXPERT, D), D_FF_EXPERT ** -0.5)

    return {"x": x, "c": c, "ada_w": ada_w, "ada_b": ada_b,
            "norm_mix_g": norm_mix_g, "norm_ffn_g": norm_ffn_g, "final_g": final_g,
            "ab_w_in": ab_w_in, "sgu_v_g": sgu_v_g, "sgu_w_s": sgu_w_s, "sgu_b_s": sgu_b_s,
            "s5_lam_re": s5_lam_re, "s5_lam_im": s5_lam_im, "s5_log_dt": s5_log_dt,
            "s5_b_re": s5_b_re, "s5_b_im": s5_b_im, "s5_c_re": s5_c_re, "s5_c_im": s5_c_im,
            "s5_d": s5_d, "s5_w_glu": s5_w_glu, "ab_w_out": ab_w_out,
            "ffn_w1": ffn_w1, "ffn_w3": ffn_w3, "ffn_w2": ffn_w2,
            "mla_w_in": mla_w_in, "mla_q_norm_g": mla_q_norm_g, "mla_kv_norm_g": mla_kv_norm_g,
            "mla_w_uq": mla_w_uq, "mla_w_ukv": mla_w_ukv, "mla_w_o": mla_w_o,
            "moe_w_router": moe_w_router, "moe_w1": moe_w1, "moe_w3": moe_w3, "moe_w2": moe_w2}

def reference(x, c, ada_w, ada_b, norm_mix_g, norm_ffn_g, final_g,
              ab_w_in, sgu_v_g, sgu_w_s, sgu_b_s,
              s5_lam_re, s5_lam_im, s5_log_dt, s5_b_re, s5_b_im, s5_c_re, s5_c_im,
              s5_d, s5_w_glu, ab_w_out,
              ffn_w1, ffn_w3, ffn_w2,
              mla_w_in, mla_q_norm_g, mla_kv_norm_g, mla_w_uq, mla_w_ukv, mla_w_o,
              moe_w_router, moe_w1, moe_w3, moe_w2):
    c_act = jax.nn.silu(c)
    for layer in range(DEPTH):
        i = layer // 2
        mod = c_act @ ada_w[layer] + ada_b[layer]
        sh_m, sc_m, g_m, sh_f, sc_f, g_f = jnp.split(mod, 6, axis=-1)

        h = modulate(rmsnorm(x, norm_mix_g[layer]), sh_m, sc_m)
        if layer % 2 == 0:
            y = ab_mixer(h, ab_w_in[i], sgu_v_g[i], sgu_w_s[i], sgu_b_s[i],
                         s5_lam_re[i], s5_lam_im[i], s5_log_dt[i], s5_b_re[i], s5_b_im[i],
                         s5_c_re[i], s5_c_im[i], s5_d[i], s5_w_glu[i], ab_w_out[i])
        else:
            y = mla_mixer(h, mla_w_in[i], mla_q_norm_g[i], mla_kv_norm_g[i],
                          mla_w_uq[i], mla_w_ukv[i], mla_w_o[i])
        x = x + g_m[:, None, :] * y

        h = modulate(rmsnorm(x, norm_ffn_g[layer]), sh_f, sc_f)
        if layer % 2 == 0:
            y = swiglu(h, ffn_w1[i], ffn_w3[i], ffn_w2[i])
        else:
            y = moe_swiglu(h, moe_w_router[i], moe_w1[i], moe_w3[i], moe_w2[i])
        x = x + g_f[:, None, :] * y
    return rmsnorm(x, final_g)


_drawn_inputs = setup_inputs


def setup_inputs(seed=0):
    import zlib

    import numpy as np

    out = dict(_drawn_inputs(seed))
    spreads = {}
    factors = {'s5_lam_re': 6.733, 'mla_q_norm_g': 4.765, 'mla_kv_norm_g': 2.963}
    for name, (base, spread) in spreads.items():
        noise = np.random.default_rng([zlib.crc32(name.encode()), seed]).standard_normal(out[name].shape)
        drawn = base * np.exp(spread * noise) if base else spread * noise
        out[name] = __import__('jax').numpy.asarray(drawn.astype(out[name].dtype))
    for name, factor in factors.items():
        out[name] = (out[name] * factor).astype(out[name].dtype)
    return out
```

```python
import concourse.bass as bass
from concourse import mybir
from contextlib import ExitStack

F32 = mybir.dt.float32
I32 = mybir.dt.int32
ALU = mybir.AluOpType
ACT = mybir.ActivationFunctionType
AX = mybir.AxisListType

P = 128
D, T = 1024, 256
KD, TT = D // P, T // P
EPS = 1e-6
HEADS_A = 4
STATE, GROUPS = 64, 32
QUADS = 4
S5_TILES = 32
BATCHES = S5_TILES // 2
F_DENSE = 2816 // P
HEADS, QT, KVT = 8, 3, 2
SCALE = (128 + 64) ** -0.5
E_N = 8
F_CHUNKS = 3584 // 512
SUB = 64
SUBS = T // SUB
SLOTS, ITEM = 7, 4096
TWO_PI = 6.283185307179586
ROUND = 12582912.0
OFF = 4096.0

SIZES = ([8 * 512] * 4 + [8 * 512] * 3 + [8 * 512] * 20 + [4 * 512] + [8 * 512] * 2
         + [8 * 512, 8 * 512, 4 * 1024] * 5 + [8 * 256, 8 * 256, 2 * 1024]
         + [8 * 512, 8 * 256, 3 * 1024, 3 * 512, 4096] + [8 * 512] * 2)
I_ADA, I_B, I_U, I_V, I_ADA2, I_GLU, I_OUT, I_FFN, I_MLA, I_WO = 0, 4, 5, 6, 7, 27, 28, 30, 48, 53
I_MOE = 55
MOE_ITEMS = 3 * F_CHUNKS

COLS = {}


def _cols(table, spec):
    at = 0
    for name, n in spec:
        table[name] = (at, at + n)
        at += n
    return at


N_KEEP = _cols(COLS, [("c", 8), ("ada_b", 96), ("g_mix", 16), ("g_ffn", 16), ("g_fin", 8), ("g_sgu", 4),
                      ("d_skip", 4), ("g_q", 3), ("g_kv", 2), ("half_pi", 1), ("ident", P), ("step", 8), ("down", 8)])
COLS_A = {}
N_A = _cols(COLS_A, [("c_re", S5_TILES * 32), ("c_im", S5_TILES * 32),
                     ("lam_re", 32), ("lam_im", 32), ("log_dt", 32), ("w_s", 512), ("b_s", 512), ("iota", T)])
COLS_C = {}
N_C = _cols(COLS_C, [("cos", T), ("sin", T), ("rot", P)])
COLS_D = {}
N_D = _cols(COLS_D, [("router", 64), ("slot", SUBS * P), ("tri", P)])


def trunk(nc, x_in, keep_in, a_in, b_in, c_in, d_in, pre_in, moe_in, out, upto=4):
    ctx = ExitStack()
    with ctx:
        def sb(name, shape, dt=F32):
            return ctx.enter_context(nc.sbuf_tensor(name, shape, dt))

        def sem(name):
            return ctx.enter_context(nc.semaphore(name))

        ring = sb("ring", [P, SLOTS, ITEM])
        x = sb("x", [P, KD, T])
        sq = sb("sq", [P, KD, T])
        h = sb("h", [P, KD, T])
        keep = sb("keep", [P, N_KEEP])
        ones = sb("ones", [P, P])
        cs = sb("cs", [P, KD])
        cs_rows = sb("cs_rows", [P, KD, 32])
        mod = sb("mod", [P, 96])
        gain = sb("gain", [P, 4, KD])
        var = sb("var", [P, T])
        rstd = sb("rstd", [P, T])
        ARENA = 17008
        arena = sb("arena", [P, ARENA])
        psum = ctx.enter_context(nc.psum_tensor("psum", [P, 8, 512], F32))
        bank = [psum[:, i, :] for i in range(8)]

        def kp(name):
            a, b = COLS[name]
            return keep[:, a:b]

        ident = kp("ident")

        class Phase:

            def __init__(self):
                self.at = 0

            def cut(self, *shape):
                n = 1
                for s in shape:
                    n *= s
                v = arena[:, self.at:self.at + n]
                self.at += n
                assert self.at <= ARENA, self.at
                if len(shape) == 2:
                    v = v.rearrange("p (a b) -> p a b", a=shape[0])
                if len(shape) == 3:
                    v = v.rearrange("p (a b c) -> p a b c", a=shape[0], b=shape[1])
                return v

        ph = Phase()
        pa = ph.cut(N_A)

        def ka(name):
            a, b = COLS_A[name]
            return pa[:, a:b]

        c_re = ka("c_re").rearrange("p (a b) -> p a b", a=32)
        c_im = ka("c_im").rearrange("p (a b) -> p a b", a=32)
        w_s = ka("w_s").rearrange("p (a b) -> p a b", a=4)
        b_s = ka("b_s").rearrange("p (a b) -> p a b", a=4)
        iota_t = ka("iota")
        ua = ph.cut(4, T)
        va = ph.cut(TT, 512)
        ub = ph.cut(4, T)
        ub_rev = ph.cut(4, T)
        small = ph.cut(12, 32)
        dt, mag, th, whole_th, s1, c1, fr, fi, tmp_a, tmp_b, den, tmp_c = (small[:, i, :] for i in range(12))
        vstat = ph.cut(8)
        tab_s = ph.cut(2, 2, T)
        tab_c = ph.cut(2, 2, T)
        turn = ph.cut(2, 2, T)
        whole = ph.cut(2, T)
        part = ph.cut(2, T)
        xre = ph.cut(2, 2, T)
        xim = ph.cut(2, 2, T)
        row = ph.cut(2, P)
        b_mat = ph.cut(2, 8, P)
        ab = h
        t1, t2, zr, zi = (sq[:, 2 * i:2 * i + 2, :] for i in range(4))
        s_tmp = sq[:, 0:2, :]

        ph = Phase()
        silu_f = ph.cut(4, T)
        act_f = ph.cut(4, T)

        ph = Phase()
        pc = ph.cut(N_C)
        cos_t, sin_t, rot = (pc[:, COLS_C[n][0]:COLS_C[n][1]] for n in ("cos", "sin", "rot"))
        z = ph.cut(6, T)
        var2 = ph.cut(2, T)
        rstd2 = ph.cut(2, T)
        k_rope = ph.cut(T)
        qn = ph.cut(HEADS, T)
        qr = ph.cut(4, T)
        kn = ph.cut(HEADS, T)
        vv = ph.cut(TT, D)
        rope_tmp = ph.cut(4, T)
        probs = ph.cut(2, TT, T)
        probs_t = ph.cut(2, TT, T)
        rmax = ph.cut(2, 2)
        rsum = ph.cut(2, 2)
        rinv = ph.cut(2, 2)
        att = h

        ph = Phase()
        pd = ph.cut(N_D)
        router = pd[:, 0:64].rearrange("p (k e) -> p k e", k=KD)
        slot_no, tri = (pd[:, COLS_D[n][0]:COLS_D[n][1]] for n in ("slot", "tri"))
        h_tok = ph.cut(TT, D)
        pick = ph.cut(SUBS, TT, SUB)
        g_pick = ph.cut(SUBS, TT, P)
        spread = ph.cut(SUBS, 2 * T)
        hg = ph.cut(SUBS, KD, SUB)
        silu_e = ph.cut(SUBS, 256)
        act_e = ph.cut(SUBS, 256)
        act_t = ph.cut(SUBS, 256)
        ye = ph.cut(SUBS, 512)
        y_moe = ph.cut(KD, T)
        rt = ph.cut(14, TT, E_N)
        logit, is1, key, one1, rest, one2, taken, off_taken, gate_a, gate_b = (rt[:, i] for i in range(10))
        cnt, over = (rt[:, i, 0, :] for i in (10, 11))
        pos = ph.cut(TT, E_N + 1)
        gate = ph.cut(TT, E_N + 1)
        top = ph.cut(4, TT)
        gates = ph.cut(5, TT)
        plan = ph.cut(SUBS + 1, E_N + 1)
        plan_int = ctx.enter_context(nc.sbuf_tensor("plan_int", [1, SUBS + 1, E_N + 1], I32))

        x_in_s, keep_s, pa_s, pc_s, pd_s = (sem(n) for n in ("x_loaded", "keep_loaded", "a_loaded", "c_loaded", "d_loaded"))
        item_in = [sem(f"item_in{i}") for i in range(SLOTS)]
        items_used = sem("items_used")
        act_own, dve_own, pool_own = sem("act_own"), sem("dve_own"), sem("pool_own")
        cs_ready, ones_ready = sem("cs_ready"), sem("ones_ready")
        sq_ready, ss_ready, var_ready, rstd_ready, xn_ready, h_act, h_dve = (
            sem(n) for n in ("sq_ready", "ss_ready", "var_ready", "rstd_ready", "xn_ready", "h_act", "h_dve"))
        row_ready, row_copied = sem("row_ready"), sem("row_copied")
        col_ready, col_used, mod_ready = sem("col_ready"), sem("col_used"), sem("mod_ready")
        b_loaded = [sem("b_loaded0"), sem("b_loaded1")]
        uvb_ready, uvb_act = sem("uvb_ready"), sem("uvb_act")
        rev_ready = sem("rev_ready")
        vvar_ready, vstd_ready, v_ready = sem("vvar_ready"), sem("vstd_ready"), sem("v_ready")
        s_ready, s_used = sem("s_ready"), sem("s_used")
        exps_ready, angle_ready, sc1_ready = sem("exps_ready"), sem("angle_ready"), sem("sc1_ready")
        turn_ready, tab_ready = sem("turn_ready"), sem("tab_ready")
        cmat_ready = sem("cmat_ready")
        vw_ready, vw_used, xs_ready, c_done, yq_ready, tab_used = (
            sem(n) for n in ("vw_ready", "vw_used", "xs_ready", "c_done", "yq_ready", "tab_used"))
        gelu_ready, glu_ready, sig_ready, ab_ready = (sem(n) for n in ("gelu_ready", "glu_ready", "sig_ready", "ab_ready"))
        proj_ready, x_updated = sem("proj_ready"), sem("x_updated")
        up_ready, silu_ready, actf_ready, down_done = (sem(n) for n in ("up_ready", "silu_ready", "actf_ready", "down_done"))
        z_ready, z_act, zsq_ready, zss_ready, zvar_ready, zstd_ready, lat_ready = (
            sem(n) for n in ("z_ready", "z_act", "zsq_ready", "zss_ready", "zvar_ready", "zstd_ready", "lat_ready"))
        rk_done, rq_done, qk_mm, qk_act, qk_dve, rope_ready = (
            sem(n) for n in ("rk_done", "rq_done", "qk_mm", "qk_act", "qk_dve", "rope_ready"))
        score_ready, max_ready, exp_ready, probs_ready, pt_mm, pt_ready, o_mm, o_ready = (
            sem(n) for n in ("score_ready", "max_ready", "exp_ready", "probs_ready", "pt_mm", "pt_ready", "o_mm", "o_ready"))
        logit_mm, taken_ready, pos_mm, gexp_ready, gdiff_ready, plan_ready, route_ready = (
            sem(n) for n in ("logit_mm", "taken_ready", "pos_mm", "gexp_ready", "gdiff_ready", "plan_ready", "route_ready"))
        tok_mm, tok_act, tok_dve = sem("tok_mm"), sem("tok_act"), sem("tok_dve")

        def sems(name):
            return [sem(f"{name}{i}") for i in range(SUBS)]

        pick_ready, hg_mm, hg_ready, g_ready, spread_mm, spread_ready = (
            sems(n) for n in ("pick_ready", "hg_mm", "hg_ready", "g_ready", "spread_mm", "spread_ready"))
        e_up, e_silu, e_act, e_turned, e_copied, e_down, ye_ready, back_mm = (
            sems(n) for n in ("e_up", "e_silu", "e_act", "e_turned", "e_copied", "e_down", "ye_ready", "back_mm"))
        y_added = sem("y_added")
        stored = sem("stored")

        block = ctx.enter_context(nc.Block())

        ADA_OF = [(4 + b + b // 4, 2 if b % 4 == 3 else 1) for b in range(BATCHES)]

        SS_BANK = [2, 4, 0, 6, 0]
        N_NORM = {1: 1, 2: 2, 3: 3, 4: 4}[upto]

        def job_out(job):
            if job < 4:
                return qn[:, 2 * job:2 * job + 2, :]
            if job < 6:
                return qr[:, 2 * (job - 4):2 * (job - 4) + 2, :]
            if job < 10:
                return kn[:, 2 * (job - 6):2 * (job - 6) + 2, :]
            return vv[:, (job - 10) // 2, ((job - 10) % 2) * 512:((job - 10) % 2) * 512 + 512]

        def plan_of(eng, b):
            return (eng.value_load(plan_int[0:1, 0, bass.ds(b, 1)], min_val=1, max_val=SUBS),
                    [b] + [eng.value_load(plan_int[0:1, s, bass.ds(b, 1)], min_val=0, max_val=E_N) for s in range(1, SUBS)])

        def for_subs(eng, of, body):
            n_subs, n = of

            def rest_of(s):
                with eng.If(n_subs > s):
                    body(s, n[s])
                    if s + 1 < SUBS:
                        rest_of(s + 1)

            body(0, n[0])
            rest_of(1)

        def u_bank(c, s):
            return 2 if s == 1 else c % 2

        TURN_BANK, GATHER_BANK, SUM_BANK, BACK_BANK = 3, 1, 4, (3, 2, 3, 2)

        @block.sync
        def _(eng):
            eng.dma_start(keep[:, :], keep_in).then_inc(keep_s, 16)
            eng.dma_start(x[:, :, :], x_in).then_inc(x_in_s, 16)
            limit = [0, 30, 48, 55, 55][upto]
            for i in range(limit):
                if i >= SLOTS:
                    eng.wait_ge(items_used, i - SLOTS + 1)
                n = SIZES[i]
                eng.dma_start(ring[:, i % SLOTS, 0:n], pre_in[i, :, 0:n]).then_inc(item_in[i % SLOTS], 16)
                if i == 3:
                    eng.dma_start(pa, a_in).then_inc(pa_s, 16)
            if upto == 4:
                def expert_items(e, b):
                    for m in range(MOE_ITEMS):
                        i = I_MOE + m
                        eng.wait_ge(items_used, b * MOE_ITEMS + (i - SLOTS + 1))
                        eng.dma_start(ring[:, i % SLOTS, :], moe_in[e, m]).then_inc(item_in[i % SLOTS], 16)

                expert_items(0, 0)
                with eng.Fori(1, E_N) as b:
                    expert_items(b, b)
            eng.wait_ge(h_dve, N_NORM + 1)
            eng.dma_start(out, h[:, :, :]).then_inc(stored, 16)
            eng.wait_ge(stored, 16)

        @block.gpsimd
        def _(eng):
            own = [0]

            def link(ins):
                own[0] += 1
                ins.then_inc(pool_own, 1)
                eng.wait_ge(pool_own, own[0])

            eng.dma_start(b_mat[:, 0], b_in[0]).then_inc(b_loaded[0], 16)
            eng.wait_ge(pa_s, 16)
            eng.wait_ge(angle_ready, 1)
            for b in range(BATCHES):
                q, dr, jp = b // 4, (b // 2) % 2, b % 2
                n = b // 2 + 1
                if b % 2 == 0 and n < BATCHES // 2:
                    if n >= 2:
                        eng.wait_ge(vw_ready, 2 * (n - 1))
                    eng.dma_start(b_mat[:, n % 2], b_in[n]).then_inc(b_loaded[n % 2], 16)
                tiles = [dr * 16 + q * 4 + 2 * jp + i for i in range(2)]
                for i, t in enumerate(tiles):
                    ins = eng.tensor_scalar(part[:, i, :], iota_t, th[:, t:t + 1], None, ALU.mult)
                link(ins)
                link(eng.tensor_scalar(whole, part, ROUND, ROUND, ALU.add, ALU.subtract))
                if b >= 2:
                    eng.wait_ge(tab_ready, b - 1)
                eng.tensor_tensor(turn[:, b % 2], part, whole, ALU.subtract).then_inc(turn_ready, 1)
                eng.wait_ge(turn_ready, b + 1)
            if upto >= 3:
                eng.wait_ge(x_updated, 2 * KD)
                eng.dma_start(pc, c_in).then_inc(pc_s, 16)
            if upto == 4:
                eng.wait_ge(x_updated, 3 * KD)
                eng.dma_start(pd, d_in).then_inc(pd_s, 16)

        @block.scalar
        def _(eng):
            own = [0]

            def link(ins):
                own[0] += 1
                ins.then_inc(act_own, 1)
                eng.wait_ge(act_own, own[0])

            def copy_row(a):
                eng.wait_ge(row_ready, a + 1)
                if a >= 2:
                    eng.wait_ge(col_ready, a - 1)
                eng.activation(row[:, a % 2, :], bank[a % 2][:, 0:P], ACT.Copy).then_inc(row_copied, 1)

            def norm(n, final=False):
                if n == 0:
                    eng.wait_ge(x_in_s, 16)
                else:
                    eng.wait_ge(x_updated, KD * n)
                eng.activation(sq[:, :, :], x[:, :, :], ACT.Square).then_inc(sq_ready, 1)
                if n == 0:
                    return
                norm_root(n)
                norm_apply(n, final)

            def norm_root(n):
                eng.wait_ge(var_ready, n + 1)
                eng.activation(rstd[:, :], var[:, :], ACT.Sqrt).then_inc(rstd_ready, 1)

            def norm_apply(n, final=False):
                if final:
                    return
                eng.wait_ge(xn_ready, n + 1)
                eng.wait_ge(mod_ready, 1 + (n > 0))
                sh = (n // 2) * 48 + (n % 2) * 24
                for k in range(0, KD, 2):
                    ins = eng.activation(h[:, k, :], sq[:, k, :], ACT.Identity, bias=mod[:, sh + k:sh + k + 1],
                                         scale=gain[:, n, k:k + 1])
                ins.then_inc(h_act, 1)

            eng.wait_ge(keep_s, 16)
            link(eng.activation(cs[:, :], kp("c"), ACT.Silu))
            eng.activation(cs_rows[:, :, :], cs[:, :].unsqueeze(2).to_broadcast([P, KD, 32]), ACT.Copy).then_inc(cs_ready, 1)
            norm(0)
            for a in range(4):
                copy_row(a)
            norm_root(0)
            norm_apply(0)
            eng.wait_ge(pa_s, 16)
            link(eng.activation(dt, ka("log_dt"), ACT.Exp))
            eng.wait_ge(sc1_ready, 1)
            eng.activation(mag, tmp_a, ACT.Exp).then_inc(exps_ready, 1)
            eng.wait_ge(angle_ready, 1)
            eng.activation(s1, th, ACT.Sin, scale=TWO_PI)
            link(eng.activation(tmp_b, th, ACT.Abs))
            eng.activation(c1, tmp_b, ACT.Sin, bias=kp("half_pi"), scale=-TWO_PI).then_inc(exps_ready, 1)
            def tables(b):
                eng.wait_ge(turn_ready, b + 1)
                if b >= 2:
                    eng.wait_ge(tab_used, b - 1)
                link(eng.activation(tab_s[:, b % 2], turn[:, b % 2], ACT.Sin, scale=TWO_PI))
                link(eng.activation(turn[:, b % 2], turn[:, b % 2], ACT.Abs))
                eng.activation(tab_c[:, b % 2], turn[:, b % 2], ACT.Sin, bias=kp("half_pi"), scale=-TWO_PI)\
                    .then_inc(tab_ready, 1)

            for i in range(2):
                eng.wait_ge(uvb_ready, i + 1)
                eng.activation(ub[:, 2 * i:2 * i + 2, :], bank[6 + i].rearrange("p (a b) -> p a b", a=2), ACT.Copy)\
                    .then_inc(uvb_act, 1)
            tables(0)
            tables(1)
            for i in range(2):
                eng.wait_ge(uvb_ready, i + 3)
                eng.activation(ua[:, 2 * i:2 * i + 2, :], bank[6 + i].rearrange("p (a b) -> p a b", a=2),
                               ACT.Gelu_apprx_tanh).then_inc(uvb_act, 1)
            for i in range(2):
                eng.wait_ge(uvb_ready, i + 5)
                eng.activation(va[:, i, :], bank[6 + i], ACT.Gelu_apprx_tanh).then_inc(uvb_act, 1)
            eng.wait_ge(vvar_ready, 1)
            eng.activation(vstat, vstat, ACT.Sqrt).then_inc(vstd_ready, 1)

            for b in range(BATCHES):
                for i in range(ADA_OF[b][1]):
                    copy_row(ADA_OF[b][0] + i)
                if b + 2 < BATCHES:
                    tables(b + 2)
            eng.wait_ge(yq_ready, QUADS)
            eng.activation(ab[:, 4:8, :], ab[:, 4:8, :], ACT.Gelu_apprx_tanh).then_inc(gelu_ready, 1)
            for i in range(2):
                eng.wait_ge(glu_ready, i + 1)
                eng.activation(ub[:, 2 * i:2 * i + 2, :], bank[2 + i][:, :].rearrange("p (a b) -> p a b", a=2),
                               ACT.Sigmoid).then_inc(sig_ready, 1)

            norm(1, upto == 1)
            if upto >= 2:
                for f in range(F_DENSE):
                    eng.wait_ge(up_ready, f + 1)
                    if f >= 4:
                        eng.wait_ge(actf_ready, f - 3)
                    eng.activation(silu_f[:, f % 4, :], bank[f % 4][:, 0:T], ACT.Silu).then_inc(silu_ready, 1)
                norm(2, upto == 2)
            if upto >= 3:
                for i in range(3):
                    eng.wait_ge(z_ready, i + 1)
                    eng.activation(z[:, 2 * i:2 * i + 2, :], bank[1 + i][:, :].rearrange("p (a b) -> p a b", a=2),
                                   ACT.Copy).then_inc(z_act, 1)
                eng.wait_ge(z_act, 3)
                eng.activation(sq[:, 0:5, :], z[:, 0:5, :], ACT.Square).then_inc(zsq_ready, 1)
                eng.wait_ge(zvar_ready, 1)
                eng.activation(rstd2, var2, ACT.Sqrt).then_inc(zstd_ready, 1)
                for job in range(0, 14, 2):
                    eng.wait_ge(qk_mm, job + 1)
                    eng.activation(job_out(job), bank[job % 4][:, :] if job >= 10 else
                                   bank[job % 4][:, :].rearrange("p (a b) -> p a b", a=2), ACT.Copy).then_inc(qk_act, 1)
                for hd in range(HEADS + 1):
                    if hd < HEADS:
                        eng.wait_ge(max_ready, hd + 1)
                        if hd >= 2:
                            eng.wait_ge(pt_mm, hd - 1)
                        for i in range(TT):
                            ins = eng.activation(probs[:, hd % 2, i, :], bank[hd % 2][:, i * T:(i + 1) * T], ACT.Exp,
                                                 bias=rmax[:, hd % 2, i:i + 1], scale=SCALE,
                                                 accum_out=rsum[:, hd % 2, i:i + 1])
                        ins.then_inc(exp_ready, 1)
                    if hd >= 1:
                        g = hd - 1
                        eng.wait_ge(pt_mm, g + 1)
                        if g >= 2:
                            eng.wait_ge(o_mm, g - 1)
                        eng.activation(probs_t[:, g % 2], bank[2 + g % 2][:, :].rearrange("p (a b) -> p a b", a=2),
                                       ACT.Copy).then_inc(pt_ready, 1)
                norm(3, upto == 3)
            if upto == 4:
                for i in range(0, 4, 2):
                    eng.wait_ge(tok_mm, i + 1)
                    eng.activation(h_tok[:, i // 2, (i % 2) * 512:(i % 2) * 512 + 512], bank[i][:, :], ACT.Copy).then_inc(tok_act, 1)
                eng.wait_ge(gdiff_ready, 1)
                eng.activation(gates[:, 1, :], gates[:, 0, :], ACT.Exp).then_inc(gexp_ready, 1)
                eng.wait_ge(plan_ready, 1)

                def gathered(s, n):
                    eng.wait_ge(hg_mm[s], n + 1)
                    eng.activation(hg[:, s], bank[GATHER_BANK].rearrange("p (a b) -> p a b", a=KD), ACT.Copy)\
                        .then_inc(hg_ready[s], 1)

                for_subs(eng, plan_of(eng, 0), gathered)
                with eng.Fori(0, E_N) as b:
                    now, then = plan_of(eng, b), plan_of(eng, b + 1)

                    def silu(s, n, c):
                        eng.wait_ge(e_up[s], n * F_CHUNKS + c + 1)
                        eng.activation(silu_e[:, s, :], bank[u_bank(c, s)][:, 0:256], ACT.Silu).then_inc(e_silu[s], 1)

                    def spread_out(s, n):
                        eng.wait_ge(spread_mm[s], n + 1)
                        eng.activation(spread[0:64, s, 0:T], bank[SUM_BANK + s][0:64, 0:T], ACT.Copy)
                        eng.activation(spread[64:128, s, T:2 * T], bank[SUM_BANK + s][64:128, 0:T], ACT.Copy)\
                            .then_inc(spread_ready[s], 1)

                    def turned(s, n, c):
                        eng.wait_ge(e_turned[s], n * F_CHUNKS + c + 1)
                        eng.activation(act_t[:, s, :], bank[TURN_BANK][:, 0:256], ACT.Copy).then_inc(e_copied[s], 1)

                    for_subs(eng, now, lambda s, n: silu(s, n, 0))
                    for_subs(eng, now, spread_out)
                    for c in range(F_CHUNKS - 1):
                        def both(s, n):
                            turned(s, n, c)
                            silu(s, n, c + 1)

                        for_subs(eng, now, both)
                    for_subs(eng, now, lambda s, n: turned(s, n, F_CHUNKS - 1))
                    for_subs(eng, then, gathered)
                norm(4, True)

        @block.vector
        def _(eng):
            own = [0]

            def link(ins):
                own[0] += 1
                ins.then_inc(dve_own, 1)
                eng.wait_ge(dve_own, own[0])

            def norm(n, final=False):
                eng.wait_ge(ss_ready, n + 1)
                link(eng.tensor_scalar(var[:, :], bank[SS_BANK[n]][:, 0:T], 1.0 / D, EPS, ALU.mult, ALU.add))
                eng.reciprocal(var[:, :], var[:, :]).then_inc(var_ready, 1)
                if n == 0:
                    return
                norm_apply(n, final)

            def norm_apply(n, final=False):
                eng.wait_ge(rstd_ready, n + 1)
                eng.tensor_tensor(sq[:, :, :], x[:, :, :], rstd[:, :].unsqueeze(1).to_broadcast([P, KD, T]), ALU.mult)\
                    .then_inc(xn_ready, 1)
                eng.wait_ge(xn_ready, n + 1)
                if final:
                    for k in range(KD):
                        ins = eng.tensor_scalar(h[:, k, :], sq[:, k, :], kp("g_fin")[:, k:k + 1], None, ALU.mult)
                else:
                    sh = (n // 2) * 48 + (n % 2) * 24
                    for k in range(1, KD, 2):
                        ins = eng.tensor_scalar(h[:, k, :], sq[:, k, :], gain[:, n, k:k + 1], mod[:, sh + k:sh + k + 1],
                                                ALU.mult, ALU.add)
                ins.then_inc(h_dve, 1)

            def make_gain(n):
                sc = (n // 2) * 48 + (n % 2) * 24 + 8
                g = kp("g_mix" if n % 2 == 0 else "g_ffn")[:, (n // 2) * 8:(n // 2) * 8 + 8]
                return eng.scalar_tensor_tensor(gain[:, n, :], mod[:, sc:sc + 8], 1.0, g, ALU.add, ALU.mult)

            def residual(count, gate_at, base_bank, ready, done):
                for m in range(KD):
                    eng.wait_ge(ready, done(m))
                    eng.scalar_tensor_tensor(x[:, m, :], bank[base_bank + m // 2][:, (m % 2) * T:(m % 2) * T + T],
                                             mod[:, gate_at + m:gate_at + m + 1], x[:, m, :], ALU.mult, ALU.add)\
                        .then_inc(x_updated, 1)

            def take_columns(a):
                eng.wait_ge(col_ready, a + 1)
                eng.tensor_tensor(mod[:, 4 * a:4 * a + 4], bank[a % 2][:, P:2 * P:32], kp("ada_b")[:, 4 * a:4 * a + 4],
                                  ALU.add).then_inc(col_used, 1)
                eng.wait_ge(col_used, a + 1)

            eng.memset(ones[:, :], 1.0).then_inc(ones_ready, 1)
            eng.wait_ge(keep_s, 16)
            norm(0)
            for a in range(4):
                take_columns(a)
            link(make_gain(0))
            eng.sem_inc(mod_ready, 1)
            norm_apply(0)
            eng.wait_ge(pa_s, 16)
            eng.wait_ge(act_own, 2)
            eng.tensor_tensor(tmp_a, ka("lam_re"), dt, ALU.mult).then_inc(sc1_ready, 1)
            link(eng.tensor_tensor(th, ka("lam_im"), dt, ALU.mult))
            link(eng.tensor_scalar(th, th, 1.0 / TWO_PI, None, ALU.mult))
            link(eng.tensor_scalar(whole_th, th, ROUND, ROUND, ALU.add, ALU.subtract))
            eng.tensor_tensor(th, th, whole_th, ALU.subtract).then_inc(angle_ready, 1)
            def output_matrices():
                eng.wait_ge(exps_ready, 2)
                link(eng.tensor_tensor(s1, s1, mag, ALU.mult))
                link(eng.tensor_tensor(c1, c1, mag, ALU.mult))
                link(eng.tensor_scalar(c1, c1, 1.0, None, ALU.subtract))
                lr, li = ka("lam_re"), ka("lam_im")
                link(eng.tensor_tensor(tmp_a, lr, lr, ALU.mult))
                link(eng.tensor_tensor(tmp_b, li, li, ALU.mult))
                link(eng.tensor_tensor(den, tmp_a, tmp_b, ALU.add))
                link(eng.reciprocal(den, den))
                link(eng.tensor_tensor(tmp_a, c1, lr, ALU.mult))
                link(eng.tensor_tensor(tmp_b, s1, li, ALU.mult))
                link(eng.tensor_tensor(tmp_a, tmp_a, tmp_b, ALU.add))
                link(eng.tensor_tensor(fr, tmp_a, den, ALU.mult))
                link(eng.tensor_tensor(tmp_a, s1, lr, ALU.mult))
                link(eng.tensor_tensor(tmp_b, c1, li, ALU.mult))
                link(eng.tensor_tensor(tmp_a, tmp_a, tmp_b, ALU.subtract))
                link(eng.tensor_tensor(fi, tmp_a, den, ALU.mult))
                w1 = sq[:, 0:4, :].rearrange("p a (b c) -> p (a b) c", c=32)
                w2 = sq[:, 4:8, :].rearrange("p a (b c) -> p (a b) c", c=32)
                frb = fr.unsqueeze(2).to_broadcast([P, 32, 32])
                fib = fi.unsqueeze(2).to_broadcast([P, 32, 32])
                link(eng.tensor_tensor(w1, c_re, frb, ALU.mult))
                link(eng.tensor_tensor(w2, c_re, fib, ALU.mult))
                link(eng.tensor_tensor(c_re, c_im, fib, ALU.mult))
                link(eng.tensor_tensor(c_re, w1, c_re, ALU.subtract))
                link(eng.tensor_tensor(c_im, c_im, frb, ALU.mult))
                eng.scalar_tensor_tensor(c_im, c_im, -1.0, w2, ALU.mult, ALU.subtract).then_inc(cmat_ready, 1)
                eng.wait_ge(cmat_ready, 1)
            def norm_v():
                eng.wait_ge(uvb_act, 6)
                vsq = sq[:, 0:4, :].rearrange("p a (b c) -> p (a b) c", c=P)
                v8 = va.rearrange("p a (b c) -> p (a b) c", c=P)
                link(eng.tensor_tensor(vsq, v8, v8, ALU.mult))
                link(eng.tensor_reduce(vstat, vsq, AX.X, ALU.add))
                link(eng.tensor_scalar(vstat, vstat, 1.0 / P, EPS, ALU.mult, ALU.add))
                eng.reciprocal(vstat, vstat).then_inc(vvar_ready, 1)
                eng.wait_ge(vstd_ready, 1)
                eng.tensor_tensor(v8, v8, vstat.unsqueeze(2).to_broadcast([P, 8, P]), ALU.mult).then_inc(v_ready, 1)

            eng.wait_ge(uvb_act, 2)
            for i in range(4):
                ins = eng.tensor_copy(ub_rev[:, i, :], ub[:, i, ::-1])
            ins.then_inc(rev_ready, 1)
            eng.wait_ge(h_act, 1)

            def gating():
                for g in range(HEADS_A):
                    eng.wait_ge(s_ready, g // 2 + 1)
                    src = bank[6 + g // 2][:, (g % 2) * T:(g % 2) * T + T].rearrange("p (a b) -> p a b", a=TT)
                    dst = s_tmp[:, g % 2, :].rearrange("p (a b) -> p a b", a=TT)
                    link(eng.scalar_tensor_tensor(dst, src, kp("g_sgu")[:, g:g + 1],
                                                  b_s[:, g, :].unsqueeze(1).to_broadcast([P, TT, P]), ALU.mult, ALU.add))
                    ins = eng.tensor_tensor(ab[:, g, :], ua[:, g, :], s_tmp[:, g % 2, :], ALU.mult)
                    link(ins)
                eng.sem_inc(s_used, 1)

            def combine(q):
                eng.wait_ge(c_done, 4 * (q + 1))
                yb = bank[6 + q % 2]
                link(eng.scalar_tensor_tensor(ab[:, 4 + q, :], ub[:, q, :], kp("d_skip")[:, q:q + 1], yb[:, 0:T],
                                              ALU.mult, ALU.add))
                eng.tensor_tensor(ab[:, 4 + q, :], ab[:, 4 + q, :], yb[:, T:2 * T][:, ::-1], ALU.add).then_inc(yq_ready, 1)
                eng.wait_ge(yq_ready, q + 1)

            for b in range(BATCHES):
                q, dr, jp = b // 4, (b // 2) % 2, b % 2
                tiles = [dr * 16 + q * 4 + 2 * jp + i for i in range(2)]
                first = 2 + 2 * (b % 2)
                v_ps = psum[:, first:first + 2, 0:T]
                w_ps = psum[:, first:first + 2, T:2 * T]
                s, c = tab_s[:, b % 2], tab_c[:, b % 2]
                eng.wait_ge(vw_ready, b + 1)
                eng.wait_ge(tab_ready, b + 1)
                eng.tensor_tensor(zr, v_ps, c, ALU.mult)
                eng.tensor_tensor(t1, w_ps, s, ALU.mult)
                eng.tensor_tensor(zi, w_ps, c, ALU.mult)
                eng.tensor_tensor(t2, v_ps, s, ALU.mult).then_inc(vw_used, 1)
                eng.wait_ge(vw_used, b + 1)
                eng.tensor_tensor(zr, zr, t1, ALU.add)
                link(eng.tensor_tensor(zi, zi, t2, ALU.subtract))
                for i, t in enumerate(tiles):
                    m = mag[:, t:t + 1].to_broadcast([P, T])
                    eng.tensor_tensor_scan(zr[:, i, :], m, zr[:, i, :], 0.0, ALU.mult, ALU.add)
                    ins = eng.tensor_tensor_scan(zi[:, i, :], m, zi[:, i, :], 0.0, ALU.mult, ALU.add)
                link(ins)
                if b >= 2:
                    eng.wait_ge(c_done, b - 1)
                eng.tensor_tensor(t1, zr, c, ALU.mult)
                link(eng.tensor_tensor(t2, zi, s, ALU.mult))
                link(eng.tensor_tensor(xre[:, b % 2], t1, t2, ALU.subtract))
                eng.tensor_tensor(t1, zr, s, ALU.mult)
                eng.tensor_tensor(t2, zi, c, ALU.mult).then_inc(tab_used, 1)
                eng.wait_ge(tab_used, b + 1)
                eng.tensor_tensor(xim[:, b % 2], t1, t2, ALU.add).then_inc(xs_ready, 1)
                eng.wait_ge(xs_ready, b + 1)
                if b == 0:
                    output_matrices()
                if b == 1:
                    norm_v()
                    gating()
                if b % 4 == 0 and b:
                    combine(b // 4 - 1)
                for i in range(ADA_OF[b][1]):
                    if b:
                        take_columns(ADA_OF[b][0] + i - 1)
            combine(QUADS - 1)
            take_columns(23)
            make_gain(1)
            make_gain(2)
            link(make_gain(3))
            eng.sem_inc(mod_ready, 1)
            eng.wait_ge(glu_ready, 2)
            for i in range(2):
                eng.wait_ge(sig_ready, i + 1)
                eng.tensor_tensor(ab[:, 4 + 2 * i:6 + 2 * i, :], ab[:, 4 + 2 * i:6 + 2 * i, :], ub[:, 2 * i:2 * i + 2, :],
                                  ALU.mult).then_inc(ab_ready, 1)
            residual(1, 16, 4, proj_ready, lambda m: m + 1)
            norm(1, upto == 1)
            if upto >= 2:
                for f in range(F_DENSE):
                    eng.wait_ge(silu_ready, f + 1)
                    if f >= 4:
                        eng.wait_ge(down_done, f - 3)
                    eng.tensor_tensor(act_f[:, f % 4, :], silu_f[:, f % 4, :], bank[f % 4][:, T:2 * T], ALU.mult)\
                        .then_inc(actf_ready, 1)
                residual(2, 40, 4, down_done, lambda m: F_DENSE)
                norm(2, upto == 2)
            if upto >= 3:
                eng.wait_ge(pc_s, 16)
                eng.wait_ge(zss_ready, 1)
                eng.tensor_scalar(var2[:, 0, :], bank[4][:, 0:T], 1.0 / (QT * P), EPS, ALU.mult, ALU.add)
                link(eng.tensor_scalar(var2[:, 1, :], bank[4][:, T:2 * T], 1.0 / (KVT * P), EPS, ALU.mult, ALU.add))
                eng.reciprocal(var2, var2).then_inc(zvar_ready, 1)
                eng.wait_ge(rk_done, 1)
                eng.tensor_tensor(rope_tmp[:, 0, :], z[:, 5, :], cos_t, ALU.mult)
                link(eng.tensor_tensor(rope_tmp[:, 1, :], bank[5][:, 0:T], sin_t, ALU.mult))
                link(eng.tensor_tensor(k_rope, rope_tmp[:, 0, :], rope_tmp[:, 1, :], ALU.add))
                eng.wait_ge(zstd_ready, 1)
                for k in range(QT + KVT):
                    g = kp("g_q")[:, k:k + 1] if k < QT else kp("g_kv")[:, k - QT:k - QT + 1]
                    ins = eng.scalar_tensor_tensor(z[:, k, :], z[:, k, :], g, rstd2[:, int(k >= QT), :], ALU.mult, ALU.mult)
                ins.then_inc(lat_ready, 1)
                for job in range(1, 14, 2):
                    eng.wait_ge(qk_mm, job + 1)
                    eng.tensor_copy(job_out(job), bank[job % 4][:, :] if job >= 10 else
                                    bank[job % 4][:, :].rearrange("p (a b) -> p a b", a=2)).then_inc(qk_dve, 1)
                eng.wait_ge(rq_done, 1)
                for i in range(2):
                    c2 = cos_t.unsqueeze(1).to_broadcast([P, 2, T])
                    s2 = sin_t.unsqueeze(1).to_broadcast([P, 2, T])
                    link(eng.tensor_tensor(rope_tmp[:, 0:2, :], qr[:, 2 * i:2 * i + 2, :], c2, ALU.mult))
                    link(eng.tensor_tensor(rope_tmp[:, 2:4, :], bank[4 + i][:, :].rearrange("p (a b) -> p a b", a=2), s2, ALU.mult))
                    link(eng.tensor_tensor(qr[:, 2 * i:2 * i + 2, :], rope_tmp[:, 0:2, :], rope_tmp[:, 2:4, :], ALU.add))
                eng.sem_inc(rope_ready, 1)
                for hd in range(HEADS + 2):
                    if hd < HEADS:
                        eng.wait_ge(score_ready, hd + 1)
                        if hd >= 2:
                            eng.wait_ge(exp_ready, hd - 1)
                        link(eng.tensor_reduce(rmax[:, hd % 2, :], bank[hd % 2][:, :].rearrange("p (a b) -> p a b", a=2),
                                               AX.X, ALU.max))
                        eng.tensor_scalar(rmax[:, hd % 2, :], rmax[:, hd % 2, :], -SCALE, None, ALU.mult).then_inc(max_ready, 1)
                        eng.wait_ge(exp_ready, hd + 1)
                        link(eng.reciprocal(rinv[:, hd % 2, :], rsum[:, hd % 2, :]))
                        for i in range(TT):
                            ins = eng.tensor_scalar(probs[:, hd % 2, i, :], probs[:, hd % 2, i, :], rinv[:, hd % 2, i:i + 1],
                                                    None, ALU.mult)
                        ins.then_inc(probs_ready, 1)
                    if hd >= 2:
                        g = hd - 2
                        eng.wait_ge(o_mm, g + 1)
                        eng.tensor_copy(att[:, g, :], bank[4 + g % 2][:, 0:T]).then_inc(o_ready, 1)
                residual(3, 64, 0, proj_ready, lambda m: KD + m + 1)
                norm(3, upto == 3)
            if upto == 4:
                eng.wait_ge(pd_s, 16)
                for i in range(1, 4, 2):
                    eng.wait_ge(tok_mm, i + 1)
                    eng.tensor_copy(h_tok[:, i // 2, (i % 2) * 512:(i % 2) * 512 + 512], bank[i][:, :]).then_inc(tok_dve, 1)
                eng.memset(spread, 0.0)
                eng.memset(y_moe, 0.0).then_inc(y_added, 1)
                eng.wait_ge(logit_mm, 1)
                b3 = [P, TT, E_N]
                down = kp("down").unsqueeze(1).to_broadcast(b3)

                def wide(v):
                    return v.unsqueeze(2).to_broadcast(b3)

                link(eng.tensor_copy(logit, bank[4][:, 0:16].rearrange("p (a b) -> p a b", a=TT)))

                def best(src, m, first):
                    link(eng.tensor_reduce(top[:, m, :], src, AX.X, ALU.max))
                    link(eng.tensor_tensor(is1, src, wide(top[:, m, :]), ALU.is_equal))
                    link(eng.tensor_tensor(key, is1, down, ALU.mult))
                    link(eng.tensor_reduce(top[:, m + 1, :], key, AX.X, ALU.max))
                    link(eng.tensor_tensor(first, key, wide(top[:, m + 1, :]), ALU.is_equal))

                best(logit, 0, one1)
                link(eng.scalar_tensor_tensor(rest, one1, -3.0e38, logit, ALU.mult, ALU.add))
                best(rest, 2, one2)
                eng.tensor_tensor(taken, one1, one2, ALU.add).then_inc(taken_ready, 1)
                eng.tensor_tensor(gates[:, 0, :], top[:, 2, :], top[:, 0, :], ALU.subtract).then_inc(gdiff_ready, 1)
                eng.wait_ge(taken_ready, 1)
                eng.tensor_scalar(off_taken, taken, -OFF, OFF, ALU.mult, ALU.add)
                eng.memset(pos[:, :, E_N:E_N + 1], OFF)
                eng.memset(gate[:, :, E_N:E_N + 1], 0.0)
                eng.memset(plan[:, 1:SUBS + 1, 0:1], 0.0)
                eng.memset(plan[:, 0, :], 1.0)
                eng.wait_ge(pos_mm, 1)
                link(eng.tensor_copy(cnt, bank[5][:, 16:24]))
                link(eng.tensor_tensor(pos[:, :, 0:E_N], bank[5][:, 0:16].rearrange("p (a b) -> p a b", a=TT), off_taken, ALU.add))

                for sub in range(1, SUBS):
                    link(eng.tensor_scalar(over, cnt, float(SUB * sub), None, ALU.is_gt))
                    link(eng.tensor_tensor(plan[:, 0, 0:E_N], plan[:, 0, 0:E_N], over, ALU.add))
                    link(eng.tensor_tensor_scan(plan[:, sub, 1:E_N + 1], kp("step"), over, 0.0, ALU.mult, ALU.add))
                link(eng.tensor_tensor_scan(plan[:, SUBS, 1:E_N + 1], kp("step"), plan[:, 0, 0:E_N], 0.0, ALU.mult, ALU.add))
                eng.tensor_copy(plan_int[0:1, :, :], plan[0:1, :, :]).then_inc(plan_ready, 1)
                eng.wait_ge(plan_ready, 1)

                def pick_of(e):
                    def body(s, n):
                        for i in range(TT):
                            ins = eng.tensor_scalar(pick[:, s, i, :], slot_no[:, s * P:s * P + SUB],
                                                    pos[:, i, bass.ds(e, 1)], None, ALU.is_equal)
                        ins.then_inc(pick_ready[s], 1)

                    return body

                for_subs(eng, plan_of(eng, 0), pick_of(0))
                eng.wait_ge(gexp_ready, 1)
                link(eng.tensor_scalar(gates[:, 2, :], gates[:, 1, :], 1.0, None, ALU.add))
                link(eng.reciprocal(gates[:, 3, :], gates[:, 2, :]))
                link(eng.tensor_tensor(gates[:, 4, :], gates[:, 3, :], gates[:, 1, :], ALU.mult))
                eng.tensor_tensor(gate_a, one1, wide(gates[:, 3, :]), ALU.mult)
                link(eng.tensor_tensor(gate_b, one2, wide(gates[:, 4, :]), ALU.mult))
                link(eng.tensor_tensor(gate[:, :, 0:E_N], gate_a, gate_b, ALU.add))
                with eng.Fori(0, E_N) as b:
                    now, then = plan_of(eng, b), plan_of(eng, b + 1)

                    def gated_pick(s, n):
                        for i in range(TT):
                            ins = eng.tensor_scalar(g_pick[:, s, i, :], slot_no[:, s * P:(s + 1) * P], pos[:, i, bass.ds(b, 1)],
                                                    gate[:, i, bass.ds(b, 1)], ALU.is_equal, ALU.mult)
                        ins.then_inc(g_ready[s], 1)

                    def product(s, n, c):
                        eng.wait_ge(e_silu[s], n * F_CHUNKS + c + 1)
                        eng.tensor_tensor(act_e[:, s, :], silu_e[:, s, :], bank[u_bank(c, s)][:, 256:512], ALU.mult)\
                            .then_inc(e_act[s], 1)

                    for_subs(eng, now, gated_pick)
                    for c in range(F_CHUNKS):
                        for_subs(eng, now, lambda s, n: product(s, n, c))
                    for_subs(eng, then, pick_of(b + 1))

                    def sum_out(s, n):
                        eng.wait_ge(e_down[s], n + 1)
                        eng.tensor_copy(ye[:, s, :], bank[SUM_BANK + s]).then_inc(ye_ready[s], 1)

                    def add_back(s, n):
                        eng.wait_ge(y_added, (earlier + s) * 4 + 1)
                        for i in range(4):
                            eng.wait_ge(back_mm[s], n * 4 + i + 1)
                            two = y_moe.rearrange("p (a b) c -> p b a c", a=2)[:, i]
                            eng.tensor_tensor(two, two, bank[BACK_BANK[i]].rearrange("p (a b) -> p a b", a=2), ALU.add)\
                                .then_inc(y_added, 1)

                    for_subs(eng, now, sum_out)
                    earlier = eng.value_load(plan_int[0:1, SUBS, bass.ds(b, 1)], min_val=0, max_val=E_N * SUBS)
                    for_subs(eng, now, add_back)
                earlier = eng.value_load(plan_int[0:1, SUBS, E_N:E_N + 1], min_val=E_N, max_val=E_N * SUBS)
                eng.wait_ge(y_added, earlier * 4 + 1)
                for m in range(KD):
                    eng.scalar_tensor_tensor(x[:, m, :], y_moe[:, m, :], mod[:, 88 + m:89 + m], x[:, m, :],
                                             ALU.mult, ALU.add).then_inc(x_updated, 1)
                norm(4, True)

        @block.tensor
        def _(eng):
            def item(i, k):
                eng.wait_ge(item_in[i % SLOTS], 16 * (i // SLOTS + 1))
                n = SIZES[i]
                return ring[:, i % SLOTS, 0:n].rearrange("p (k n) -> p k n", k=k)

            def norm_sum(n):
                eng.wait_ge(sq_ready, n + 1)
                for k in range(KD):
                    ins = eng.matmul(bank[SS_BANK[n]][:, 0:T], ones[:, :], sq[:, k, :], start=k == 0, stop=k == KD - 1)
                ins.then_inc(ss_ready, 1)

            def ada(a):
                i = a if a < 4 else I_ADA2 + a - 4
                w = item(i, KD)
                if a >= 2:
                    eng.wait_ge(col_used, a - 1)
                for k in range(KD):
                    for j in range(4):
                        ins = eng.matmul(bank[a % 2][32 * j:32 * j + 32, 0:P], cs_rows[:, k, :], w[:, k, j * P:(j + 1) * P],
                                         start=k == 0, stop=k == KD - 1, tile_position=(0, 32 * j))
                ins.then_inc(row_ready, 1)
                eng.wait_ge(row_ready, a + 1)
                eng.sem_inc(items_used, 1)

            def ada_turn(a):
                eng.wait_ge(row_copied, a + 1)
                eng.transpose(bank[a % 2][:, P:2 * P], row[:, a % 2, :], ident).then_inc(col_ready, 1)

            def h_ready(n):
                eng.wait_ge(h_act, n + 1)
                eng.wait_ge(h_dve, n + 1)

            eng.wait_ge(ones_ready, 1)
            norm_sum(0)
            eng.wait_ge(cs_ready, 1)
            for a in range(4):
                ada(a)
                if a:
                    ada_turn(a - 1)
            ada_turn(3)
            h_ready(0)

            def tiles4(i, base, ready):
                w = item(i, KD)
                for m in range(4):
                    for k in range(KD):
                        ins = eng.matmul(bank[base + m // 2][:, (m % 2) * T:(m % 2) * T + T], w[:, k, m * P:(m + 1) * P],
                                         h[:, k, :], start=k == 0, stop=k == KD - 1)
                    if m == 3:
                        ins.then_inc(items_used, 1)
                        eng.wait_ge(items_used, i + 1)
                        eng.sem_inc(ready, 1)
                    elif m == 1:
                        ins.then_inc(ready, 1)

            def b_products(b):
                q, dr, jp = b // 4, (b // 2) % 2, b % 2
                if b == 0:
                    eng.wait_ge(uvb_act, 2)
                elif b >= 2:
                    eng.wait_ge(vw_used, b - 1)
                n = b // 2
                if jp == 0:
                    eng.wait_ge(b_loaded[n % 2], 16 * (n // 2 + 1))
                if dr:
                    eng.wait_ge(rev_ready, 1)
                src = ub_rev if dr else ub
                for i in range(2):
                    for o in range(2):
                        ins = eng.matmul(bank[2 + 2 * (b % 2) + i][:, o * T:(o + 1) * T],
                                         b_mat[:, n % 2, 2 * (2 * jp + i) + o, :], src[:, q, :], start=True, stop=True)
                ins.then_inc(vw_ready, 1)

            def c_products(b):
                q, dr, jp = b // 4, (b // 2) % 2, b % 2
                eng.wait_ge(xs_ready, b + 1)
                if q >= 2 and b % 4 == 0:
                    eng.wait_ge(yq_ready, q - 1)
                for mat, xs in ((c_re, xre), (c_im, xim)):
                    for i in range(2):
                        r, t = 32 * (2 * jp + i), dr * 16 + q * 4 + 2 * jp + i
                        ins = eng.matmul(bank[6 + q % 2][r:r + 32, dr * T:(dr + 1) * T], mat[:, t, :], xs[:, b % 2, i, :],
                                         start=xs is xre, stop=xs is xim, tile_position=(0, r))
                ins.then_inc(c_done, 1)

            tiles4(I_B, 6, uvb_ready)
            b_products(0)
            b_products(1)
            tiles4(I_U, 6, uvb_ready)
            w = item(I_V, KD)
            for i in range(TT):
                eng.wait_ge(uvb_act, 3 + i)
                for k in range(KD):
                    ins = eng.matmul(bank[6 + i], h[:, k, i * P:(i + 1) * P], w[:, k, :], start=k == 0, stop=k == KD - 1)
                ins.then_inc(uvb_ready, 1)
            eng.wait_ge(uvb_ready, 6)
            eng.sem_inc(items_used, 1)
            for b in range(BATCHES):
                for i in range(ADA_OF[b][1]):
                    a = ADA_OF[b][0] + i
                    ada(a)
                    if a > 4:
                        ada_turn(a - 1)
                if b == 0:
                    eng.wait_ge(v_ready, 1)
                    for g in range(HEADS_A):
                        for i in range(TT):
                            o = (g % 2) * T + i * P
                            ins = eng.matmul(bank[6 + g // 2][:, o:o + P], va[:, i, g * P:(g + 1) * P], w_s[:, g, :],
                                             start=True, stop=True)
                        if g % 2:
                            ins.then_inc(s_ready, 1)
                    eng.wait_ge(s_used, 1)
                    eng.wait_ge(cmat_ready, 1)
                c_products(b)
                if b + 2 < BATCHES:
                    b_products(b + 2)
            ada_turn(23)
            eng.wait_ge(gelu_ready, 1)
            w = item(I_GLU, 4)
            for m in range(4):
                for k in range(4):
                    ins = eng.matmul(bank[2 + m // 2][:, (m % 2) * T:(m % 2) * T + T], w[:, k, m * P:(m + 1) * P],
                                     ab[:, 4 + k, :], start=k == 0, stop=k == 3)
                if m % 2:
                    ins.then_inc(glu_ready, 1)
            eng.wait_ge(glu_ready, 2)
            eng.sem_inc(items_used, 1)

            def project(first, src, base, count):
                for i in range(2):
                    w = item(first + i, KD)
                    for m in range(4):
                        t = 4 * i + m
                        for k in range(KD):
                            ins = eng.matmul(bank[base + t // 2][:, (t % 2) * T:(t % 2) * T + T], w[:, k, m * P:(m + 1) * P],
                                             src[:, k, :], start=k == 0, stop=k == KD - 1)
                        if t % 2:
                            ins.then_inc(proj_ready, 2)
                    eng.wait_ge(proj_ready, count + 4 * i + 4)
                    eng.sem_inc(items_used, 1)

            eng.wait_ge(ab_ready, 2)
            project(I_OUT, ab, 4, 0)
            norm_sum_wait = None
            norm_sum(1)
            if upto >= 2:
                h_ready(1)

                def up(f):
                    c, r = f // 4, f % 4
                    n = min(4, F_DENSE - 4 * c)
                    i = I_FFN + 3 * c
                    w1, w3 = item(i, KD), item(i + 1, KD)
                    if f >= 4:
                        eng.wait_ge(actf_ready, f - 3)
                    for o, w in ((0, w1), (T, w3)):
                        for k in range(KD):
                            ins = eng.matmul(bank[f % 4][:, o:o + T], w[:, k, r * P:(r + 1) * P], h[:, k, :],
                                             start=k == 0, stop=k == KD - 1)
                    ins.then_inc(up_ready, 1)
                    if r == n - 1:
                        eng.wait_ge(up_ready, f + 1)
                        eng.sem_inc(items_used, 2)

                def down(f):
                    c, r = f // 4, f % 4
                    n = min(4, F_DENSE - 4 * c)
                    w2 = item(I_FFN + 3 * c + 2, n)
                    eng.wait_ge(actf_ready, f + 1)
                    for m in range(KD):
                        ins = eng.matmul(bank[4 + m // 2][:, (m % 2) * T:(m % 2) * T + T], w2[:, r, m * P:(m + 1) * P],
                                         act_f[:, f % 4, :], start=f == 0 and m % 2 == 0, stop=f == F_DENSE - 1,
                                         skip_group_check=True)
                    ins.then_inc(down_done, 1)
                    if r == n - 1:
                        eng.wait_ge(down_done, f + 1)
                        eng.sem_inc(items_used, 1)

                up(0)
                up(1)
                for f in range(F_DENSE):
                    down(f)
                    if f + 2 < F_DENSE:
                        up(f + 2)
                norm_sum(2)
            if upto >= 3:
                h_ready(2)
                wa, wb = item(I_MLA, KD), item(I_MLA + 1, KD)
                for m in range(6):
                    w = wa[:, :, m * P:(m + 1) * P] if m < 4 else wb[:, :, (m - 4) * P:(m - 3) * P]
                    for k in range(KD):
                        ins = eng.matmul(bank[1 + m // 2][:, (m % 2) * T:(m % 2) * T + T], w[:, k, :], h[:, k, :],
                                         start=k == 0, stop=k == KD - 1)
                    if m % 2:
                        ins.then_inc(z_ready, 1)
                eng.wait_ge(z_ready, 3)
                eng.sem_inc(items_used, 2)
                eng.wait_ge(zsq_ready, 1)
                for k in range(QT):
                    eng.matmul(bank[4][:, 0:T], ones[:, :], sq[:, k, :], start=k == 0, stop=k == QT - 1)
                for k in range(KVT):
                    ins = eng.matmul(bank[4][:, T:2 * T], ones[:, :], sq[:, QT + k, :], start=k == 0, stop=k == KVT - 1)
                ins.then_inc(zss_ready, 1)
                eng.wait_ge(pc_s, 16)
                eng.matmul(bank[5][:, 0:T], rot, z[:, 5, :], start=True, stop=True).then_inc(rk_done, 1)
                eng.wait_ge(lat_ready, 1)

                def job_begin(job):
                    if job >= 4:
                        if job % 2 == 0:
                            eng.wait_ge(qk_act, job // 2 - 1)
                        else:
                            eng.wait_ge(qk_dve, job // 2 - 1)

                def two_tiles(job, w, kt, src0, col):
                    job_begin(job)
                    for i in range(2):
                        for k in range(kt):
                            ins = eng.matmul(bank[job % 4][:, i * T:(i + 1) * T], w[:, k, col + i * P:col + (i + 1) * P],
                                             z[:, src0 + k, :], start=k == 0, stop=k == kt - 1)
                    ins.then_inc(qk_mm, 1)

                w = item(I_MLA + 2, QT)
                for job in range(4):
                    two_tiles(job, w, QT, 0, job * 2 * P)
                w = item(I_MLA + 3, QT)
                for job in range(4, 6):
                    two_tiles(job, w, QT, 0, (job - 4) * 2 * P)
                eng.wait_ge(qk_mm, 6)
                eng.sem_inc(items_used, 2)
                w = item(I_MLA + 4, 4)
                for job in range(6, 10):
                    two_tiles(job, w[:, 0:2, :], KVT, QT, (job - 6) * 2 * P)
                for job in range(10, 14):
                    job_begin(job)
                    i, hf = (job - 10) // 2, (job - 10) % 2
                    for k in range(KVT):
                        ins = eng.matmul(bank[job % 4][:, :], z[:, QT + k, i * P:(i + 1) * P], w[:, 2 + k, hf * 512:hf * 512 + 512],
                                         start=k == 0, stop=k == KVT - 1)
                    ins.then_inc(qk_mm, 1)
                eng.wait_ge(qk_mm, 14)
                eng.sem_inc(items_used, 1)
                for i in range(4):
                    ins = eng.matmul(bank[4 + i // 2][:, (i % 2) * T:(i % 2) * T + T], rot, qr[:, i, :], start=True, stop=True)
                ins.then_inc(rq_done, 1)
                eng.wait_ge(rope_ready, 1)
                eng.wait_ge(qk_act, 7)
                eng.wait_ge(qk_dve, 7)

                def scores(hd):
                    if hd >= 2:
                        eng.wait_ge(exp_ready, hd - 1)
                    r = 64 * (hd % 2)
                    for i in range(TT):
                        o = bank[hd % 2][:, i * T:(i + 1) * T]
                        eng.matmul(o, qn[:, hd, i * P:(i + 1) * P], kn[:, hd, :], start=True, stop=False)
                        ins = eng.matmul(o, qr[r:r + 64, hd // 2, i * P:(i + 1) * P], k_rope[r:r + 64, :], start=False, stop=True)
                    ins.then_inc(score_ready, 1)

                def turn_probs(hd):
                    eng.wait_ge(probs_ready, hd + 1)
                    if hd >= 2:
                        eng.wait_ge(pt_ready, hd - 1)
                    for kt in range(TT):
                        for i in range(TT):
                            ins = eng.transpose(bank[2 + hd % 2][:, kt * T + i * P:kt * T + (i + 1) * P],
                                                probs[:, hd % 2, i, kt * P:(kt + 1) * P], ident)
                    ins.then_inc(pt_mm, 1)

                def values(hd):
                    eng.wait_ge(pt_ready, hd + 1)
                    if hd >= 2:
                        eng.wait_ge(o_ready, hd - 1)
                    for kt in range(TT):
                        ins = eng.matmul(bank[4 + hd % 2][:, 0:T], vv[:, kt, hd * P:(hd + 1) * P], probs_t[:, hd % 2, kt, :],
                                         start=kt == 0, stop=kt == TT - 1)
                    ins.then_inc(o_mm, 1)

                scores(0)
                for hd in range(HEADS):
                    if hd + 1 < HEADS:
                        scores(hd + 1)
                    turn_probs(hd)
                    if hd:
                        values(hd - 1)
                values(HEADS - 1)
                eng.wait_ge(o_ready, HEADS)
                project(I_WO, att, 0, KD)
                norm_sum(3)
            if upto == 4:
                h_ready(3)
                for i in range(4):
                    tt, hf = i // 2, i % 2
                    for k in range(4):
                        ins = eng.transpose(bank[i][:, k * P:(k + 1) * P], h[:, hf * 4 + k, tt * P:(tt + 1) * P], ident)
                    ins.then_inc(tok_mm, 1)
                eng.wait_ge(pd_s, 16)
                for i in range(TT):
                    for k in range(KD):
                        ins = eng.matmul(bank[4][:, i * 8:i * 8 + 8], h[:, k, i * P:(i + 1) * P], router[:, k, :],
                                         start=k == 0, stop=k == KD - 1)
                ins.then_inc(logit_mm, 1)
                eng.wait_ge(taken_ready, 1)
                eng.matmul(bank[5][:, 0:8], tri, taken[:, 0, :], start=True, stop=True)
                eng.matmul(bank[5][:, 8:16], ones[:, :], taken[:, 0, :], start=True, stop=False)
                eng.matmul(bank[5][:, 8:16], tri, taken[:, 1, :], start=False, stop=True)
                eng.matmul(bank[5][:, 16:24], ones[:, :], taken[:, 0, :], start=True, stop=False)
                eng.matmul(bank[5][:, 16:24], ones[:, :], taken[:, 1, :], start=False, stop=True).then_inc(pos_mm, 1)
                eng.wait_ge(tok_act, 2)
                eng.wait_ge(tok_dve, 2)
                eng.wait_ge(plan_ready, 1)

                def gather(s, n, of):
                    eng.wait_ge(pick_ready[s], n + 1)
                    if s:
                        eng.wait_ge(hg_ready[s - 1], of[1][s - 1] + 1)
                    for k in range(KD):
                        for i in range(TT):
                            ins = eng.matmul(bank[GATHER_BANK][:, k * SUB:(k + 1) * SUB], h_tok[:, i, k * P:(k + 1) * P],
                                             pick[:, s, i, :], start=i == 0, stop=i == TT - 1)
                    ins.then_inc(hg_mm[s], 1)

                first = plan_of(eng, 0)
                for_subs(eng, first, lambda s, n: gather(s, n, first))
                with eng.Fori(0, E_N) as b:
                    now, then = plan_of(eng, b), plan_of(eng, b + 1)
                    earlier = eng.value_load(plan_int[0:1, SUBS, bass.ds(b, 1)], min_val=0, max_val=E_N * SUBS)

                    def e_item(m, k):
                        i = I_MOE + m
                        eng.wait_ge(item_in[i % SLOTS], b * (16 * MOE_ITEMS // SLOTS) + 16 * (i // SLOTS + 1))
                        return ring[:, i % SLOTS, :].rearrange("p (k n) -> p k n", k=k)

                    def turn(s, n, c):
                        eng.wait_ge(e_act[s], n * F_CHUNKS + c + 1)
                        if s:
                            eng.wait_ge(e_copied[s - 1], now[1][s - 1] * F_CHUNKS + c + 1)
                        for q in range(2):
                            ins = eng.transpose(bank[TURN_BANK][:, q * P:(q + 1) * P], act_e[:, s, q * P:(q + 1) * P], ident)
                        ins.then_inc(e_turned[s], 1)

                    def up(s, n, c, used):
                        if c == 0:
                            eng.wait_ge(hg_ready[s], n + 1)
                        if s >= 2:
                            before = 0 if s == 2 else 2
                            eng.wait_ge(e_act[before], now[1][before] * F_CHUNKS + c + 1)
                        if s == 1:
                            if c:
                                eng.wait_ge(e_act[s], n * F_CHUNKS + c)
                            else:
                                eng.wait_ge(y_added, earlier * 4 + 1)
                        for o, m in ((0, UP_ITEM[c]), (256, UP_ITEM[c] + 1)):
                            w = e_item(m, KD)
                            for k in range(KD):
                                for j in range(2):
                                    ins = eng.matmul(bank[u_bank(c, s)][64 * j:64 * j + 64, o:o + 256], hg[:, s, k, :],
                                                     w[:, k, 256 * j:256 * j + 256], start=k == 0, stop=k == KD - 1,
                                                     tile_position=(0, 64 * j))
                                    if s == 0 and used and o == 0 and k == 0 and j == 0:
                                        ins.then_inc(items_used, used)
                            if o == 0 and c:
                                turn(s, n, c - 1)
                        ins.then_inc(e_up[s], 1)

                    def down(s, n, c, used):
                        w = e_item(DOWN_ITEM[c], 4)
                        eng.wait_ge(e_copied[s], n * F_CHUNKS + c + 1)
                        if c == 0:
                            eng.wait_ge(spread_ready[s], n + 1)
                        for t in range(4):
                            for j in range(2):
                                ins = eng.matmul(bank[SUM_BANK + s][64 * j:64 * j + 64, :],
                                                 act_t[:, s, (t % 2) * P + (t // 2) * 64:(t % 2) * P + (t // 2) * 64 + 64],
                                                 w[:, t, 512 * j:512 * j + 512], start=c == 0 and t == 0,
                                                 stop=c == F_CHUNKS - 1 and t == 3, tile_position=(0, 64 * j))
                                if s == 0 and t == 0 and j == 0:
                                    ins.then_inc(items_used, used)
                        if c == F_CHUNKS - 1:
                            ins.then_inc(e_down[s], 1)

                    def spread_turn(s, n):
                        eng.wait_ge(g_ready[s], n + 1)
                        for i in range(TT):
                            ins = eng.transpose(bank[SUM_BANK + s][:, i * P:(i + 1) * P], g_pick[:, s, i, :], ident)
                        ins.then_inc(spread_mm[s], 1)

                    def back(s, n):
                        eng.wait_ge(ye_ready[s], n + 1)
                        for i in range(4):
                            if s or i >= 2:
                                eng.wait_ge(y_added, (earlier + s) * 4 + i)
                            for j in range(2):
                                ins = eng.matmul(bank[BACK_BANK[i]][:, j * T:(j + 1) * T], ye[:, s, i * P:(i + 1) * P],
                                                 spread[:, s, j * T:(j + 1) * T], start=True, stop=True)
                                if s == 0 and i == 0 and j == 0:
                                    ins.then_inc(items_used, 1)
                            ins.then_inc(back_mm[s], 1)

                    for_subs(eng, now, lambda s, n: up(s, n, 0, 0))
                    for_subs(eng, now, spread_turn)
                    eng.wait_ge(y_added, earlier * 4 + 1)
                    for c in range(F_CHUNKS - 1):
                        for_subs(eng, now, lambda s, n: up(s, n, c + 1, 2 if c == 0 else 1))
                        for_subs(eng, now, lambda s, n: down(s, n, c, 2))
                    for_subs(eng, now, lambda s, n: turn(s, n, F_CHUNKS - 1))
                    for_subs(eng, then, lambda s, n: gather(s, n, then))
                    for_subs(eng, now, lambda s, n: down(s, n, F_CHUNKS - 1, 1))
                    for_subs(eng, now, back)
                norm_sum(4)


UP_ITEM, DOWN_ITEM, MOE_ORDER = [], [], []
for _c in range(F_CHUNKS + 1):
    if _c < F_CHUNKS:
        UP_ITEM.append(len(MOE_ORDER))
        MOE_ORDER += [("w1", _c), ("w3", _c)]
    if _c:
        DOWN_ITEM.append(len(MOE_ORDER))
        MOE_ORDER += [("w2", _c - 1)]


def layout(inp):
    import numpy as np

    f = np.float32
    a = {k: np.asarray(v) for k, v in inp.items()}

    def col(v):
        return np.asarray(v, f).reshape(-1, P).T

    def tiles(w, n):
        k = w.shape[0] // P
        return w.reshape(k, P, w.shape[1]).transpose(1, 0, 2).reshape(P, -1)

    out = {}
    out["x"] = np.ascontiguousarray(a["x"][0].T.reshape(KD, P, T).transpose(1, 0, 2))
    keep = np.zeros((P, N_KEEP), f)

    def put(dst, table, name, v):
        s, e = table[name]
        dst[:, s:e] = v

    put(keep, COLS, "c", col(a["c"][0]))
    put(keep, COLS, "ada_b", col(a["ada_b"].reshape(-1)))
    put(keep, COLS, "g_mix", col(a["norm_mix_g"].reshape(-1)))
    put(keep, COLS, "g_ffn", col(a["norm_ffn_g"].reshape(-1)))
    put(keep, COLS, "g_fin", col(a["final_g"]))
    put(keep, COLS, "g_sgu", a["sgu_v_g"][0].T)
    put(keep, COLS, "d_skip", col(a["s5_d"][0]))
    put(keep, COLS, "g_q", col(a["mla_q_norm_g"][0]))
    put(keep, COLS, "g_kv", col(a["mla_kv_norm_g"][0]))
    put(keep, COLS, "half_pi", np.pi / 2)
    put(keep, COLS, "ident", np.eye(P, dtype=f))
    put(keep, COLS, "step", 1.0)
    put(keep, COLS, "down", np.arange(E_N, 0, -1, dtype=f)[None, :])
    out["keep"] = keep

    pa = np.zeros((P, N_A), f)
    m = np.zeros((4, 2, 4, 2, 16, 4, 2, 2, STATE), f)
    for n, src in enumerate((a["s5_b_re"][0], a["s5_b_im"][0])):
        s = src.reshape(2, 4, 4, 2, STATE, 16)
        for pr in range(4):
            for g in range(2):
                m[:, :, pr, g, :, pr, n, g, :] = s[:, :, pr, g].transpose(1, 0, 3, 2)
    out["pb"] = m.reshape(8, P, 8, P)
    for name, src in (("c_re", a["s5_c_re"][0]), ("c_im", a["s5_c_im"][0])):
        m = np.zeros((2, STATE, S5_TILES, 2, 16), f)
        s = src.reshape(S5_TILES, 2, 16, STATE)
        for g in range(2):
            m[g, :, :, g, :] = s[:, g].transpose(2, 0, 1)
        put(pa, COLS_A, name, m.reshape(P, -1))
    put(pa, COLS_A, "lam_re", a["s5_lam_re"][0].reshape(S5_TILES, P).T)
    put(pa, COLS_A, "lam_im", a["s5_lam_im"][0].reshape(S5_TILES, P).T)
    put(pa, COLS_A, "log_dt", np.repeat(a["s5_log_dt"][0].reshape(S5_TILES, 2).T, STATE, axis=0))
    put(pa, COLS_A, "w_s", a["sgu_w_s"][0].transpose(2, 0, 1).reshape(P, -1))
    put(pa, COLS_A, "b_s", np.broadcast_to(a["sgu_b_s"][0].reshape(1, -1), (P, 512)))
    put(pa, COLS_A, "iota", np.arange(T, dtype=f)[None, :])
    out["pa"] = pa

    pc = np.zeros((P, N_C), f)
    inv = 10000.0 ** (-np.arange(0, 64, 2, dtype=f) / f(64))
    ang = np.arange(T, dtype=f)[None, :] * inv.astype(f)[:, None]
    put(pc, COLS_C, "cos", np.tile(np.cos(ang), (4, 1)))
    put(pc, COLS_C, "sin", np.tile(np.concatenate([-np.sin(ang), np.sin(ang)]), (2, 1)))
    rot = np.zeros((P, P), f)
    for r in range(P):
        rot[r ^ 32, r] = 1.0
    put(pc, COLS_C, "rot", rot)
    out["pc"] = pc

    pd = np.zeros((P, N_D), f)
    put(pd, COLS_D, "router", tiles(a["moe_w_router"][0], 8))
    put(pd, COLS_D, "slot", (np.arange(SUBS)[:, None] * SUB + np.arange(P)[None, :] % SUB).reshape(1, -1))
    put(pd, COLS_D, "tri", np.triu(np.ones((P, P), f), 1))
    out["pd"] = pd

    pre = np.zeros((I_MOE, P, ITEM), f)

    def item(i, w):
        pre[i, :, 0:w.shape[1]] = w

    for layer in range(2):
        for j in range(12):
            n = layer * 12 + j
            item(n if n < 4 else I_ADA2 + n - 4, tiles(a["ada_w"][layer][:, j * 512:(j + 1) * 512], 512))
    for j, i in enumerate((I_U, I_V, I_B)):
        item(i, tiles(a["ab_w_in"][0][:, j * 512:(j + 1) * 512], 512))
    item(I_GLU, tiles(a["s5_w_glu"][0], 512))
    for j in range(2):
        item(I_OUT + j, tiles(a["ab_w_out"][0][:, j * 512:(j + 1) * 512], 512))
        item(I_WO + j, tiles(a["mla_w_o"][0][:, j * 512:(j + 1) * 512], 512))
    for j in range(6):
        cut = slice(j * 512, min((j + 1) * 512, F_DENSE * P))
        item(I_FFN + 3 * j, tiles(a["ffn_w1"][0][:, cut], 512))
        item(I_FFN + 3 * j + 1, tiles(a["ffn_w3"][0][:, cut], 512))
        item(I_FFN + 3 * j + 2, tiles(a["ffn_w2"][0][cut], D))
    w = a["mla_w_in"][0]
    item(I_MLA, tiles(w[:, 0:512], 512))
    item(I_MLA + 1, tiles(np.concatenate([w[:, 512:640], w[:, 640:704], w[:, 640:704]], axis=1), 256))
    uq = a["mla_w_uq"][0].reshape(-1, HEADS, 192)
    item(I_MLA + 2, tiles(uq[:, :, 0:128].reshape(-1, 1024), 1024))
    item(I_MLA + 3, tiles(uq[:, :, 128:192].reshape(-1, 512), 512))
    ukv = a["mla_w_ukv"][0].reshape(-1, HEADS, 256)
    item(I_MLA + 4, np.concatenate([tiles(ukv[:, :, 0:128].reshape(-1, 1024), 1024),
                                    tiles(ukv[:, :, 128:256].reshape(-1, 1024), 1024)], axis=1))
    out["pre"] = pre

    moe = np.zeros((E_N, MOE_ITEMS, P, ITEM), f)
    for n, (which, c) in enumerate(MOE_ORDER):
        w = a["moe_" + which][0]
        if which == "w2":
            moe[:, n] = w[:, c * 512:(c + 1) * 512].reshape(E_N, 4, P, D).transpose(0, 2, 1, 3).reshape(E_N, P, ITEM)
        else:
            moe[:, n] = w[:, :, c * 512:(c + 1) * 512].reshape(E_N, KD, P, 512).transpose(0, 2, 1, 3).reshape(E_N, P, ITEM)
    out["moe"] = moe
    return out


def program(nc, shapes, upto=4):
    args = [nc.dram_tensor(f"in_{n}", s, F32, kind="ExternalInput").ap() for n, s in shapes.items()]
    out = nc.dram_tensor("out_0", (P, KD, T), F32, kind="ExternalOutput").ap()
    trunk(nc, *args, out, upto=upto)


def kernel(**inputs):
    import numpy as np
    import concourse.bacc as bacc
    from concourse.bass_utils import run_bass_kernel_spmd

    arrays = layout(inputs)
    nc = bacc.Bacc("TRN2", target_bir_lowering=False, num_devices=1)
    program(nc, {n: arrays[n].shape for n in ("x", "keep", "pa", "pb", "pc", "pd", "pre", "moe")})
    r = run_bass_kernel_spmd(nc, [{f"in_{n}": v for n, v in arrays.items()}], core_ids=[0])
    y = np.asarray(r.results[0]["out_0"])
    return np.ascontiguousarray(y.transpose(1, 0, 2).reshape(D, T).T).reshape(1, T, D)
```

```python
import concourse.bass as bass
from concourse import mybir
from contextlib import ExitStack

F32 = mybir.dt.float32
F32R = mybir.dt.float32r
I32 = mybir.dt.int32
ALU = mybir.AluOpType
ACT = mybir.ActivationFunctionType
AX = mybir.AxisListType

P = 128
D, T = 1024, 256
KD, TT = D // P, T // P
EPS = 1e-6
HEADS_A = 4
STATE = 64
QUADS = 4
S5_TILES = 32
BATCHES = S5_TILES // 2
F_DENSE = 2816 // P
HEADS, QT, KVT = 8, 3, 2
SCALE = (128 + 64) ** -0.5
E_N = 8
F_CHUNKS = 3584 // 512
SUB = 64
SUBS = T // SUB
SLOTS, ITEM = 7, 4096
N_NORMS = 5
TWO_PI = 6.283185307179586
ROUND = 12582912.0
OFF = 4096.0

SIZES = ([8 * 512] * 4 + [8 * 512] * 3 + [8 * 512] * 16 + [4 * 512] + [8 * 512] * 6
         + [8 * 512, 8 * 512, 4 * 1024] * 5 + [8 * 256, 8 * 256, 2 * 1024]
         + [8 * 512, 8 * 256, 3 * 1024, 3 * 512, 4096] + [8 * 512] * 2)
I_B, I_U, I_V, I_GLU, I_OUT, I_FFN, I_MLA, I_WO = 4, 5, 6, 23, (25, 27), 30, 48, (53, 54)
I_ADA = [0, 1, 2, 3] + list(range(7, 23)) + [24, 26, 28, 29]
I_MOE = 55
MOE_ITEMS = 3 * F_CHUNKS

COLS = {}


def _cols(table, spec):
    at = 0
    for name, n in spec:
        table[name] = (at, at + n)
        at += n
    return at


N_KEEP = _cols(COLS, [("c", 8), ("ada_b", 96), ("g_mix", 16), ("g_ffn", 16), ("g_fin", 8), ("g_sgu", 4),
                      ("d_skip", 4), ("g_q", 3), ("g_kv", 2), ("half_pi", 1), ("ident", P), ("step", 8), ("down", 8)])
COLS_A = {}
N_A = _cols(COLS_A, [("c_re", S5_TILES * 32), ("c_im", S5_TILES * 32),
                     ("lam_re", 32), ("lam_im", 32), ("log_dt", 32), ("w_s", 512), ("b_s", 512), ("iota", T)])
COLS_C = {}
N_C = _cols(COLS_C, [("cos", T), ("sin", T), ("rot", P)])
COLS_D = {}
N_D = _cols(COLS_D, [("router", 64), ("slot", SUBS * P), ("tri", P)])


def trunk(nc, x_in, keep_in, a_in, b_in, c_in, d_in, pre_in, moe_in, out):
    ctx = ExitStack()
    with ctx:
        place = {}

        def sb(name, shape, dt=F32):
            place[name] = (nc.sbuf_base + 31) // 32 * 32
            return ctx.enter_context(nc.sbuf_tensor(name, shape, dt))

        def rounded(name, shape, skip=0):
            return nc.alloc_sbuf_tensor_at(f"{name}_r{skip}", shape, F32R, offset=place[name] + 4 * skip)

        def sem(name):
            return ctx.enter_context(nc.semaphore(name))

        ring = sb("ring", [P, SLOTS, ITEM])
        x = sb("x", [P, KD, T])
        sq = sb("sq", [P, KD, T])
        h = sb("h", [P, KD, T])
        keep = sb("keep", [P, N_KEEP])
        ones = sb("ones", [P, P])
        cs = sb("cs", [P, KD])
        cs_rows = sb("cs_rows", [P, KD, 32])
        mod = sb("mod", [P, 96])
        gain = sb("gain", [P, 4, KD])
        var = sb("var", [P, T])
        rstd = sb("rstd", [P, T])
        ARENA = 17008
        arena = sb("arena", [P, ARENA])
        ring_r = [rounded("ring", [P, ITEM], i * ITEM) for i in range(SLOTS)]
        sq_r, h_r = rounded("sq", [P, KD, T]), rounded("h", [P, KD, T])
        arena_r = rounded("arena", [P, ARENA])
        psum = ctx.enter_context(nc.psum_tensor("psum", [P, 8, 512], F32))
        bank = [psum[:, i, :] for i in range(8)]

        def kp(name):
            a, b = COLS[name]
            return keep[:, a:b]

        ident = kp("ident")

        class Phase:

            def __init__(self):
                self.at = 0

            def cut(self, *shape, whole=arena):
                n = 1
                for s in shape:
                    n *= s
                v = whole[:, self.at:self.at + n]
                self.at += n
                assert self.at <= ARENA, self.at
                if len(shape) == 2:
                    v = v.rearrange("p (a b) -> p a b", a=shape[0])
                if len(shape) == 3:
                    v = v.rearrange("p (a b c) -> p a b c", a=shape[0], b=shape[1])
                return v

        ph = Phase()
        pa = ph.cut(N_A)

        def ka(name):
            a, b = COLS_A[name]
            return pa[:, a:b]

        c_re = ka("c_re").rearrange("p (a b) -> p a b", a=32)
        c_im = ka("c_im").rearrange("p (a b) -> p a b", a=32)
        w_s = ka("w_s").rearrange("p (a b) -> p a b", a=4)
        b_s = ka("b_s").rearrange("p (a b) -> p a b", a=4)
        iota_t = ka("iota")
        ua = ph.cut(4, T)
        va = ph.cut(TT, 512)
        ub = ph.cut(4, T)
        ub_rev = ph.cut(4, T)
        small = ph.cut(11, 32)
        dt, mag, th, whole_th, s1, c1, fr, fi, tmp_a, tmp_b, den = (small[:, i, :] for i in range(11))
        vstat = ph.cut(8)
        tab_s = ph.cut(2, 2, T)
        tab_c = ph.cut(2, 2, T)
        turn = ph.cut(2, 2, T)
        whole = ph.cut(2, T)
        part = ph.cut(2, T)
        xs_re = [ph.cut(2, 2, T), ph.cut(2, 2, T)]
        xs_im = [tab_s, tab_c]
        row = ph.cut(2, P)
        b_mat = ph.cut(2, 8, P)
        ab = h
        t1, t2, zr, zi = (sq[:, 2 * i:2 * i + 2, :] for i in range(4))
        s_tmp = sq[:, 0:2, :]

        ph = Phase()
        silu_f = ph.cut(4, T)
        act_f = ph.cut(4, T)
        act_hi = ph.cut(4, T, whole=arena_r)
        act_lo = ph.cut(4, T, whole=arena_r)
        w_hi = ph.cut(4, 3, 1024, whole=arena_r)
        h_hi, h_lo = sq_r, h_r

        ph = Phase()
        pc = ph.cut(N_C)
        cos_t, sin_t, rot = (pc[:, COLS_C[n][0]:COLS_C[n][1]] for n in ("cos", "sin", "rot"))
        z = ph.cut(6, T)
        var2 = ph.cut(2, T)
        rstd2 = ph.cut(2, T)
        k_rope = ph.cut(T)
        qn = ph.cut(HEADS, T)
        qr = ph.cut(4, T)
        kn = ph.cut(HEADS, T)
        vv = ph.cut(TT, D)
        rope_tmp = ph.cut(4, T)
        probs = ph.cut(2, TT, T)
        probs_t = ph.cut(2, TT, T)
        rmax = ph.cut(2, 2)
        rsum = ph.cut(2, 2)
        rinv = ph.cut(2, 2)
        att = h

        ph = Phase()
        pd = ph.cut(N_D)
        router = pd[:, 0:64].rearrange("p (k e) -> p k e", k=KD)
        slot_no, tri = (pd[:, COLS_D[n][0]:COLS_D[n][1]] for n in ("slot", "tri"))
        h_tok = ph.cut(TT, D)
        pick = ph.cut(SUBS, TT, SUB)
        g_pick = ph.cut(SUBS, TT, P)
        spread = ph.cut(SUBS, 2 * T)
        hg = ph.cut(SUBS, KD, SUB)
        silu_e = ph.cut(SUBS, 256)
        act_e = ph.cut(SUBS, 256)
        act_t = ph.cut(SUBS, 256)
        ye = ph.cut(SUBS, 512)
        y_moe = ph.cut(KD, T)
        rt = ph.cut(14, TT, E_N)
        logit, is1, key, one1, rest, one2, taken, off_taken, gate_a, gate_b = (rt[:, i] for i in range(10))
        cnt, over = (rt[:, i, 0, :] for i in (10, 11))
        pos = ph.cut(TT, E_N + 1)
        gate = ph.cut(TT, E_N + 1)
        top = ph.cut(4, TT)
        gates = ph.cut(5, TT)
        plan = ph.cut(SUBS + 1, E_N + 1)
        plan_int = ctx.enter_context(nc.sbuf_tensor("plan_int", [1, SUBS + 1, E_N + 1], I32))

        x_in_s, keep_s, pa_s, pc_s, pd_s = (sem(n) for n in ("x_loaded", "keep_loaded", "a_loaded", "c_loaded", "d_loaded"))
        item_in = [sem(f"item_in{i}") for i in range(SLOTS)]
        items_used = sem("items_used")
        act_own, dve_own, pool_own = sem("act_own"), sem("dve_own"), sem("pool_own")
        cs_ready, ones_ready = sem("cs_ready"), sem("ones_ready")
        sq_ready, ss_ready, var_ready, rstd_ready, xn_ready, h_act, h_dve = (
            sem(n) for n in ("sq_ready", "ss_ready", "var_ready", "rstd_ready", "xn_ready", "h_act", "h_dve"))
        row_ready, row_copied = sem("row_ready"), sem("row_copied")
        col_ready, col_used, mod_ready = sem("col_ready"), sem("col_used"), sem("mod_ready")
        b_loaded = [sem("b_loaded0"), sem("b_loaded1")]
        uvb_ready, uvb_act = sem("uvb_ready"), sem("uvb_act")
        rev_ready = sem("rev_ready")
        vvar_ready, vstd_ready, v_ready = sem("vvar_ready"), sem("vstd_ready"), sem("v_ready")
        s_ready, s_used = sem("s_ready"), sem("s_used")
        exps_ready, angle_ready, sc1_ready = sem("exps_ready"), sem("angle_ready"), sem("sc1_ready")
        turn_ready, tab_ready = sem("turn_ready"), sem("tab_ready")
        cmat_ready = sem("cmat_ready")
        vw_ready, vw_used, xs_ready, c_done, yq_ready = (
            sem(n) for n in ("vw_ready", "vw_used", "xs_ready", "c_done", "yq_ready"))
        gelu_ready, glu_ready, sig_ready, ab_ready = (sem(n) for n in ("gelu_ready", "glu_ready", "sig_ready", "ab_ready"))
        proj_ready, x_updated = sem("proj_ready"), sem("x_updated")
        whi_ready, wlo_ready, hhi_ready, hlo_ready = (sem(n) for n in ("whi_ready", "wlo_ready", "hhi_ready", "hlo_ready"))
        up_ready, silu_ready, actf_ready, down_done = (sem(n) for n in ("up_ready", "silu_ready", "actf_ready", "down_done"))
        z_ready, z_act, zsq_ready, zss_ready, zvar_ready, zstd_ready, lat_ready = (
            sem(n) for n in ("z_ready", "z_act", "zsq_ready", "zss_ready", "zvar_ready", "zstd_ready", "lat_ready"))
        rk_done, rq_done, qk_mm, qk_act, qk_dve, rope_ready = (
            sem(n) for n in ("rk_done", "rq_done", "qk_mm", "qk_act", "qk_dve", "rope_ready"))
        score_ready, max_ready, exp_ready, probs_ready, pt_mm, pt_ready, o_mm, o_ready = (
            sem(n) for n in ("score_ready", "max_ready", "exp_ready", "probs_ready", "pt_mm", "pt_ready", "o_mm", "o_ready"))
        logit_mm, taken_ready, pos_mm, gexp_ready, gdiff_ready, plan_ready = (
            sem(n) for n in ("logit_mm", "taken_ready", "pos_mm", "gexp_ready", "gdiff_ready", "plan_ready"))
        tok_mm, tok_act = sem("tok_mm"), sem("tok_act")

        def sems(name):
            return [sem(f"{name}{i}") for i in range(SUBS)]

        pick_ready, hg_mm, hg_ready, g_ready, spread_mm, spread_ready = (
            sems(n) for n in ("pick_ready", "hg_mm", "hg_ready", "g_ready", "spread_mm", "spread_ready"))
        e_up, e_silu, e_act, e_turned, e_copied, e_down, ye_ready, back_mm = (
            sems(n) for n in ("e_up", "e_silu", "e_act", "e_turned", "e_copied", "e_down", "ye_ready", "back_mm"))
        y_added = sem("y_added")
        stored = sem("stored")

        block = ctx.enter_context(nc.Block())

        SS_BANK = [2, 4, 0, 6, 0]

        def job_out(job):
            if job < 4:
                return qn[:, 2 * job:2 * job + 2, :]
            if job < 6:
                return qr[:, 2 * (job - 4):2 * (job - 4) + 2, :]
            if job < 10:
                return kn[:, 2 * (job - 6):2 * (job - 6) + 2, :]
            return vv[:, (job - 10) // 2, ((job - 10) % 2) * 512:((job - 10) % 2) * 512 + 512]

        def plan_of(eng, b):
            return (eng.value_load(plan_int[0:1, 0, bass.ds(b, 1)], min_val=1, max_val=SUBS),
                    [b] + [eng.value_load(plan_int[0:1, s, bass.ds(b, 1)], min_val=0, max_val=E_N) for s in range(1, SUBS)])

        def for_subs(eng, of, body, later_only=False):
            n_subs, n = of

            def rest_of(s):
                with eng.If(n_subs > s):
                    body(s, n[s])
                    if s + 1 < SUBS:
                        rest_of(s + 1)

            if not later_only:
                body(0, n[0])
            rest_of(1)

        def u_bank(c, s):
            return 2 if s == 1 else c % 2

        TURN_BANK, GATHER_BANK, SUM_BANK, BACK_BANK = 3, 1, 4, (3, 2, 3, 2)

        def ffn_piece(f, n, slots=None):
            c, r = f // 4, f % 4
            i = I_FFN + 3 * c + n
            v = slots[i % SLOTS][:, 0:SIZES[i]] if slots else ring[:, i % SLOTS, 0:SIZES[i]]
            if n == 2:
                return i, v[:, r * D:(r + 1) * D]
            return i, v.rearrange("p (k n) -> p k n", k=KD)[:, :, r * P:(r + 1) * P]

        def hi_piece(f, n):
            v = w_hi[:, f % 4, n, :]
            return v if n == 2 else v.rearrange("p (k n) -> p k n", k=KD)

        @block.sync
        def _(eng):
            eng.dma_start(keep[:, :], keep_in).then_inc(keep_s, 16)
            eng.dma_start(x[:, :, :], x_in).then_inc(x_in_s, 16)
            for i in range(I_MOE):
                if i >= SLOTS:
                    eng.wait_ge(items_used, i - SLOTS + 1)
                n = SIZES[i]
                eng.dma_start(ring[:, i % SLOTS, 0:n], pre_in[i, :, 0:n]).then_inc(item_in[i % SLOTS], 16)
                if i == 3:
                    eng.dma_start(pa, a_in).then_inc(pa_s, 16)
            def expert_items(e, b):
                for m in range(MOE_ITEMS):
                    i = I_MOE + m
                    eng.wait_ge(items_used, b * MOE_ITEMS + (i - SLOTS + 1))
                    eng.dma_start(ring[:, i % SLOTS, :], moe_in[e, m]).then_inc(item_in[i % SLOTS], 16)

            expert_items(0, 0)
            with eng.Fori(1, E_N) as b:
                expert_items(b, b)
            eng.wait_ge(h_dve, 2 * N_NORMS)
            eng.dma_start(out, h[:, :, :]).then_inc(stored, 16)
            eng.wait_ge(stored, 16)

        @block.gpsimd
        def _(eng):
            own = [0]

            def link(ins):
                own[0] += 1
                ins.then_inc(pool_own, 1)
                eng.wait_ge(pool_own, own[0])

            eng.dma_start(b_mat[:, 0], b_in[0]).then_inc(b_loaded[0], 16)
            eng.wait_ge(pa_s, 16)
            eng.wait_ge(angle_ready, 1)
            for b in range(BATCHES):
                q, dr, jp = b // 4, (b // 2) % 2, b % 2
                n = b // 2 + 1
                if b % 2 == 0 and n < BATCHES // 2:
                    if n >= 2:
                        eng.wait_ge(vw_ready, 2 * (n - 1))
                    eng.dma_start(b_mat[:, n % 2], b_in[n]).then_inc(b_loaded[n % 2], 16)
                tiles = [dr * 16 + q * 4 + 2 * jp + i for i in range(2)]
                for i, t in enumerate(tiles):
                    ins = eng.tensor_scalar(part[:, i, :], iota_t, th[:, t:t + 1], None, ALU.mult)
                link(ins)
                link(eng.tensor_scalar(whole, part, ROUND, ROUND, ALU.add, ALU.subtract))
                if b >= 2:
                    eng.wait_ge(tab_ready, b - 1)
                eng.tensor_tensor(turn[:, b % 2], part, whole, ALU.subtract).then_inc(turn_ready, 1)
                eng.wait_ge(turn_ready, b + 1)
            eng.wait_ge(x_updated, 2 * KD)
            eng.dma_start(pc, c_in).then_inc(pc_s, 16)
            eng.wait_ge(x_updated, 3 * KD)
            eng.dma_start(pd, d_in).then_inc(pd_s, 16)
            eng.memset(spread, 0.0)
            eng.memset(y_moe, 0.0).then_inc(y_added, 1)

        @block.scalar
        def _(eng):
            own = [0]

            def link(ins):
                own[0] += 1
                ins.then_inc(act_own, 1)
                eng.wait_ge(act_own, own[0])

            def copy_row(a):
                eng.wait_ge(row_ready, a + 1)
                if a >= 2:
                    eng.wait_ge(col_ready, a - 1)
                eng.activation(row[:, a % 2, :], bank[a % 2][:, 0:P], ACT.Copy).then_inc(row_copied, 1)

            def norm(n, final=False):
                for k in range(0, KD, 2):
                    if n == 0:
                        eng.wait_ge(x_in_s, 16)
                    else:
                        eng.wait_ge(x_updated, KD * (n - 1) + k + 2)
                    eng.activation(sq[:, k:k + 2, :], x[:, k:k + 2, :], ACT.Square).then_inc(sq_ready, 1)
                if n == 0:
                    return
                norm_root(n)
                norm_apply(n, final)

            def norm_root(n):
                eng.wait_ge(var_ready, n + 1)
                eng.activation(rstd[:, :], var[:, :], ACT.Sqrt).then_inc(rstd_ready, 1)

            def norm_apply(n, final=False):
                if final:
                    return
                eng.wait_ge(mod_ready, (1, 2, 2, 3)[n])
                sh = (n // 2) * 48 + (n % 2) * 24
                for k in range(0, KD, 2):
                    if k % 4 == 0:
                        eng.wait_ge(xn_ready, 2 * n + (2 if k else 1))
                    ins = eng.activation(h[:, k, :], sq[:, k, :], ACT.Identity, bias=mod[:, sh + k:sh + k + 1],
                                         scale=gain[:, n, k:k + 1])
                    if k % 4:
                        ins.then_inc(h_act, 1)

            eng.wait_ge(keep_s, 16)
            link(eng.activation(cs[:, :], kp("c"), ACT.Silu))
            eng.activation(cs_rows[:, :, :], cs[:, :].unsqueeze(2).to_broadcast([P, KD, 32]), ACT.Copy).then_inc(cs_ready, 1)
            norm(0)
            for a in range(4):
                copy_row(a)
            norm_root(0)
            norm_apply(0)
            eng.wait_ge(pa_s, 16)
            link(eng.activation(dt, ka("log_dt"), ACT.Exp))
            eng.wait_ge(sc1_ready, 1)
            eng.activation(mag, tmp_a, ACT.Exp).then_inc(exps_ready, 1)
            eng.wait_ge(angle_ready, 1)
            eng.activation(s1, th, ACT.Sin, scale=TWO_PI)
            link(eng.activation(tmp_b, th, ACT.Abs))
            eng.activation(c1, tmp_b, ACT.Sin, bias=kp("half_pi"), scale=-TWO_PI).then_inc(exps_ready, 1)
            def tables(b):
                eng.wait_ge(turn_ready, b + 1)
                if b >= 2:
                    eng.wait_ge(c_done, b - 1)
                link(eng.activation(tab_s[:, b % 2], turn[:, b % 2], ACT.Sin, scale=TWO_PI))
                link(eng.activation(turn[:, b % 2], turn[:, b % 2], ACT.Abs))
                eng.activation(tab_c[:, b % 2], turn[:, b % 2], ACT.Sin, bias=kp("half_pi"), scale=-TWO_PI)\
                    .then_inc(tab_ready, 1)

            for i in range(2):
                eng.wait_ge(uvb_ready, i + 1)
                eng.activation(ub[:, 2 * i:2 * i + 2, :], bank[6 + i].rearrange("p (a b) -> p a b", a=2), ACT.Copy)\
                    .then_inc(uvb_act, 1)
            tables(0)
            tables(1)
            for i in range(2):
                eng.wait_ge(uvb_ready, i + 3)
                eng.activation(ua[:, 2 * i:2 * i + 2, :], bank[6 + i].rearrange("p (a b) -> p a b", a=2),
                               ACT.Gelu_apprx_tanh).then_inc(uvb_act, 1)
            for i in range(2):
                eng.wait_ge(uvb_ready, i + 5)
                eng.activation(va[:, i, :], bank[6 + i], ACT.Gelu_apprx_tanh).then_inc(uvb_act, 1)
            eng.wait_ge(vvar_ready, 1)
            eng.activation(vstat, vstat, ACT.Sqrt).then_inc(vstd_ready, 1)

            for b in range(BATCHES):
                copy_row(4 + b)
                if b + 2 < BATCHES:
                    tables(b + 2)
            eng.wait_ge(yq_ready, QUADS)
            eng.activation(ab[:, 4:8, :], ab[:, 4:8, :], ACT.Gelu_apprx_tanh).then_inc(gelu_ready, 1)
            for i in range(2):
                eng.wait_ge(glu_ready, i + 1)
                eng.activation(ub[:, 2 * i:2 * i + 2, :], bank[2 + i][:, :].rearrange("p (a b) -> p a b", a=2),
                               ACT.Sigmoid).then_inc(sig_ready, 1)
            def high_parts(f):
                if f >= 4:
                    eng.wait_ge(down_done, f - 3)
                for n in range(3):
                    i, w = ffn_piece(f, n)
                    if f % 4 == 0:
                        eng.wait_ge(item_in[i % SLOTS], 16 * (i // SLOTS + 1))
                    eng.activation(hi_piece(f, n), w, ACT.Copy).then_inc(whi_ready, 1)

            copy_row(20)
            copy_row(21)
            eng.wait_ge(ab_ready, 2)
            high_parts(0)
            high_parts(1)
            norm(1)
            for i in range(2):
                eng.wait_ge(h_act, 3 + i)
                eng.wait_ge(h_dve, 3 + i)
                eng.activation(h_hi[:, 4 * i:4 * i + 4, :], h[:, 4 * i:4 * i + 4, :], ACT.Copy).then_inc(hhi_ready, 1)
            copy_row(22)
            copy_row(23)
            high_parts(2)
            for f in range(F_DENSE):
                eng.wait_ge(up_ready, f + 1)
                if f >= 4:
                    eng.wait_ge(actf_ready, f - 3)
                eng.activation(silu_f[:, f % 4, :], bank[f % 4][:, 0:T], ACT.Silu).then_inc(silu_ready, 1)
                if f + 3 < F_DENSE:
                    high_parts(f + 3)
            norm(2)
            for i in range(3):
                eng.wait_ge(z_ready, i + 1)
                eng.activation(z[:, 2 * i:2 * i + 2, :], bank[1 + i][:, :].rearrange("p (a b) -> p a b", a=2),
                               ACT.Copy).then_inc(z_act, 1)
            eng.wait_ge(z_act, 3)
            eng.activation(sq[:, 0:5, :], z[:, 0:5, :], ACT.Square).then_inc(zsq_ready, 1)
            eng.wait_ge(zvar_ready, 1)
            eng.activation(rstd2, var2, ACT.Sqrt).then_inc(zstd_ready, 1)
            for job in range(0, 14, 2):
                eng.wait_ge(qk_mm, job + 1)
                eng.activation(job_out(job), bank[job % 4][:, :] if job >= 10 else
                               bank[job % 4][:, :].rearrange("p (a b) -> p a b", a=2), ACT.Copy).then_inc(qk_act, 1)
            for hd in range(HEADS + 1):
                if hd < HEADS:
                    eng.wait_ge(max_ready, hd + 1)
                    if hd >= 2:
                        eng.wait_ge(pt_mm, hd - 1)
                    for i in range(TT):
                        ins = eng.activation(probs[:, hd % 2, i, :], bank[hd % 2][:, i * T:(i + 1) * T], ACT.Exp,
                                             bias=rmax[:, hd % 2, i:i + 1], scale=SCALE,
                                             accum_out=rsum[:, hd % 2, i:i + 1])
                    ins.then_inc(exp_ready, 1)
                if hd >= 1:
                    g = hd - 1
                    eng.wait_ge(pt_mm, g + 1)
                    if g >= 2:
                        eng.wait_ge(o_mm, g - 1)
                    eng.activation(probs_t[:, g % 2], bank[2 + g % 2][:, :].rearrange("p (a b) -> p a b", a=2),
                                   ACT.Copy).then_inc(pt_ready, 1)
            norm(3)
            for i in range(4):
                eng.wait_ge(tok_mm, i + 1)
                eng.activation(h_tok[:, i // 2, (i % 2) * 512:(i % 2) * 512 + 512], bank[i][:, :], ACT.Copy).then_inc(tok_act, 1)
            eng.wait_ge(gdiff_ready, 1)
            eng.activation(gates[:, 1, :], gates[:, 0, :], ACT.Exp).then_inc(gexp_ready, 1)

            def gathered(s, n):
                eng.wait_ge(hg_mm[s], n + 1)
                eng.activation(hg[:, s], bank[GATHER_BANK].rearrange("p (a b) -> p a b", a=KD), ACT.Copy)\
                    .then_inc(hg_ready[s], 1)

            gathered(0, 0)
            eng.wait_ge(y_added, 1)
            eng.wait_ge(plan_ready, 1)
            for_subs(eng, plan_of(eng, 0), gathered, later_only=True)
            with eng.Fori(0, E_N) as b:
                now, then = plan_of(eng, b), plan_of(eng, b + 1)

                def silu(s, n, c):
                    eng.wait_ge(e_up[s], n * F_CHUNKS + c + 1)
                    eng.activation(silu_e[:, s, :], bank[u_bank(c, s)][:, 0:256], ACT.Silu).then_inc(e_silu[s], 1)

                def spread_out(s, n):
                    eng.wait_ge(spread_mm[s], n + 1)
                    eng.activation(spread[0:64, s, 0:T], bank[SUM_BANK + s][0:64, 0:T], ACT.Copy)
                    eng.activation(spread[64:128, s, T:2 * T], bank[SUM_BANK + s][64:128, 0:T], ACT.Copy)\
                        .then_inc(spread_ready[s], 1)

                def turned(s, n, c):
                    eng.wait_ge(e_turned[s], n * F_CHUNKS + c + 1)
                    eng.activation(act_t[:, s, :], bank[TURN_BANK][:, 0:256], ACT.Copy).then_inc(e_copied[s], 1)

                for_subs(eng, now, lambda s, n: silu(s, n, 0))
                for_subs(eng, now, spread_out)
                for c in range(F_CHUNKS - 1):
                    def both(s, n):
                        turned(s, n, c)
                        silu(s, n, c + 1)

                    for_subs(eng, now, both)
                for_subs(eng, now, lambda s, n: turned(s, n, F_CHUNKS - 1))
                for_subs(eng, then, gathered)
            norm(4, True)

        @block.vector
        def _(eng):
            own = [0]

            def link(ins):
                own[0] += 1
                ins.then_inc(dve_own, 1)
                eng.wait_ge(dve_own, own[0])

            def norm(n, final=False):
                eng.wait_ge(ss_ready, n + 1)
                link(eng.tensor_scalar(var[:, :], bank[SS_BANK[n]][:, 0:T], 1.0 / D, EPS, ALU.mult, ALU.add))
                eng.reciprocal(var[:, :], var[:, :]).then_inc(var_ready, 1)
                if n == 0:
                    return
                norm_apply(n, final)

            def norm_apply(n, final=False):
                eng.wait_ge(rstd_ready, n + 1)
                for g in (0, KD // 2):
                    eng.tensor_tensor(sq[:, g:g + 4, :], x[:, g:g + 4, :], rstd[:, :].unsqueeze(1).to_broadcast([P, KD // 2, T]),
                                      ALU.mult).then_inc(xn_ready, 1)
                    eng.wait_ge(xn_ready, 2 * n + (2 if g else 1))
                    sh = (n // 2) * 48 + (n % 2) * 24
                    for k in range(g, g + 4):
                        if final:
                            ins = eng.tensor_scalar(h[:, k, :], sq[:, k, :], kp("g_fin")[:, k:k + 1], None, ALU.mult)
                        elif k % 2:
                            ins = eng.tensor_scalar(h[:, k, :], sq[:, k, :], gain[:, n, k:k + 1], mod[:, sh + k:sh + k + 1],
                                                    ALU.mult, ALU.add)
                    ins.then_inc(h_dve, 1)

            def make_gain(n):
                sc = (n // 2) * 48 + (n % 2) * 24 + 8
                g = kp("g_mix" if n % 2 == 0 else "g_ffn")[:, (n // 2) * 8:(n // 2) * 8 + 8]
                return eng.scalar_tensor_tensor(gain[:, n, :], mod[:, sc:sc + 8], 1.0, g, ALU.add, ALU.mult)

            def residual(gate_at, base_bank, ready, done, start=0, end=KD):
                for m in range(start, end):
                    eng.wait_ge(ready, done(m))
                    eng.scalar_tensor_tensor(x[:, m, :], bank[base_bank + m // 2][:, (m % 2) * T:(m % 2) * T + T],
                                             mod[:, gate_at + m:gate_at + m + 1], x[:, m, :], ALU.mult, ALU.add)\
                        .then_inc(x_updated, 1)

            def take_columns(a):
                eng.wait_ge(col_ready, a + 1)
                eng.tensor_tensor(mod[:, 4 * a:4 * a + 4], bank[a % 2][:, P:2 * P:32], kp("ada_b")[:, 4 * a:4 * a + 4],
                                  ALU.add).then_inc(col_used, 1)
                eng.wait_ge(col_used, a + 1)

            eng.memset(ones[:, :], 1.0).then_inc(ones_ready, 1)
            eng.wait_ge(keep_s, 16)
            norm(0)
            for a in range(4):
                take_columns(a)
            link(make_gain(0))
            eng.sem_inc(mod_ready, 1)
            norm_apply(0)
            eng.wait_ge(pa_s, 16)
            eng.wait_ge(act_own, 2)
            eng.tensor_tensor(tmp_a, ka("lam_re"), dt, ALU.mult).then_inc(sc1_ready, 1)
            link(eng.tensor_tensor(th, ka("lam_im"), dt, ALU.mult))
            link(eng.tensor_scalar(th, th, 1.0 / TWO_PI, None, ALU.mult))
            link(eng.tensor_scalar(whole_th, th, ROUND, ROUND, ALU.add, ALU.subtract))
            eng.tensor_tensor(th, th, whole_th, ALU.subtract).then_inc(angle_ready, 1)
            def output_matrices():
                eng.wait_ge(exps_ready, 2)
                link(eng.tensor_tensor(s1, s1, mag, ALU.mult))
                link(eng.tensor_tensor(c1, c1, mag, ALU.mult))
                link(eng.tensor_scalar(c1, c1, 1.0, None, ALU.subtract))
                lr, li = ka("lam_re"), ka("lam_im")
                link(eng.tensor_tensor(tmp_a, lr, lr, ALU.mult))
                link(eng.tensor_tensor(tmp_b, li, li, ALU.mult))
                link(eng.tensor_tensor(den, tmp_a, tmp_b, ALU.add))
                link(eng.reciprocal(den, den))
                link(eng.tensor_tensor(tmp_a, c1, lr, ALU.mult))
                link(eng.tensor_tensor(tmp_b, s1, li, ALU.mult))
                link(eng.tensor_tensor(tmp_a, tmp_a, tmp_b, ALU.add))
                link(eng.tensor_tensor(fr, tmp_a, den, ALU.mult))
                link(eng.tensor_tensor(tmp_a, s1, lr, ALU.mult))
                link(eng.tensor_tensor(tmp_b, c1, li, ALU.mult))
                link(eng.tensor_tensor(tmp_a, tmp_a, tmp_b, ALU.subtract))
                link(eng.tensor_tensor(fi, tmp_a, den, ALU.mult))
                w1 = sq[:, 0:4, :].rearrange("p a (b c) -> p (a b) c", c=32)
                w2 = sq[:, 4:8, :].rearrange("p a (b c) -> p (a b) c", c=32)
                frb = fr.unsqueeze(2).to_broadcast([P, 32, 32])
                fib = fi.unsqueeze(2).to_broadcast([P, 32, 32])
                link(eng.tensor_tensor(w1, c_re, frb, ALU.mult))
                link(eng.tensor_tensor(w2, c_re, fib, ALU.mult))
                link(eng.tensor_tensor(c_re, c_im, fib, ALU.mult))
                link(eng.tensor_tensor(c_re, w1, c_re, ALU.subtract))
                link(eng.tensor_tensor(c_im, c_im, frb, ALU.mult))
                eng.scalar_tensor_tensor(c_im, c_im, -1.0, w2, ALU.mult, ALU.subtract).then_inc(cmat_ready, 1)
                eng.wait_ge(cmat_ready, 1)
            def norm_v():
                eng.wait_ge(uvb_act, 6)
                vsq = sq[:, 0:4, :].rearrange("p a (b c) -> p (a b) c", c=P)
                v8 = va.rearrange("p a (b c) -> p (a b) c", c=P)
                link(eng.tensor_tensor(vsq, v8, v8, ALU.mult))
                link(eng.tensor_reduce(vstat, vsq, AX.X, ALU.add))
                link(eng.tensor_scalar(vstat, vstat, 1.0 / P, EPS, ALU.mult, ALU.add))
                eng.reciprocal(vstat, vstat).then_inc(vvar_ready, 1)
                eng.wait_ge(vstd_ready, 1)
                eng.tensor_tensor(v8, v8, vstat.unsqueeze(2).to_broadcast([P, 8, P]), ALU.mult).then_inc(v_ready, 1)

            eng.wait_ge(h_act, 2)
            eng.wait_ge(h_dve, 2)
            output_matrices()
            eng.wait_ge(uvb_act, 2)
            for i in range(4):
                ins = eng.tensor_copy(ub_rev[:, i, :], ub[:, i, ::-1])
            ins.then_inc(rev_ready, 1)

            def gating():
                for g in range(HEADS_A):
                    eng.wait_ge(s_ready, g // 2 + 1)
                    src = bank[6 + g // 2][:, (g % 2) * T:(g % 2) * T + T].rearrange("p (a b) -> p a b", a=TT)
                    dst = s_tmp[:, g % 2, :].rearrange("p (a b) -> p a b", a=TT)
                    link(eng.scalar_tensor_tensor(dst, src, kp("g_sgu")[:, g:g + 1],
                                                  b_s[:, g, :].unsqueeze(1).to_broadcast([P, TT, P]), ALU.mult, ALU.add))
                    ins = eng.tensor_tensor(ab[:, g, :], ua[:, g, :], s_tmp[:, g % 2, :], ALU.mult)
                    link(ins)
                eng.sem_inc(s_used, 1)

            def combine(q):
                eng.wait_ge(c_done, 4 * (q + 1))
                yb = bank[6 + q % 2]
                link(eng.scalar_tensor_tensor(ab[:, 4 + q, :], ub[:, q, :], kp("d_skip")[:, q:q + 1], yb[:, 0:T],
                                              ALU.mult, ALU.add))
                eng.tensor_tensor(ab[:, 4 + q, :], ab[:, 4 + q, :], yb[:, T:2 * T][:, ::-1], ALU.add).then_inc(yq_ready, 1)
                eng.wait_ge(yq_ready, q + 1)

            for b in range(BATCHES):
                q, dr, jp = b // 4, (b // 2) % 2, b % 2
                tiles = [dr * 16 + q * 4 + 2 * jp + i for i in range(2)]
                first = 2 + 2 * (b % 2)
                v_ps = psum[:, first:first + 2, 0:T]
                w_ps = psum[:, first:first + 2, T:2 * T]
                s, c = tab_s[:, b % 2], tab_c[:, b % 2]
                eng.wait_ge(vw_ready, b + 1)
                eng.wait_ge(tab_ready, b + 1)
                eng.tensor_tensor(zr, v_ps, c, ALU.mult)
                eng.tensor_tensor(t1, w_ps, s, ALU.mult)
                eng.tensor_tensor(zi, w_ps, c, ALU.mult)
                eng.tensor_tensor(t2, v_ps, s, ALU.mult).then_inc(vw_used, 1)
                eng.wait_ge(vw_used, b + 1)
                eng.tensor_tensor(zr, zr, t1, ALU.add)
                link(eng.tensor_tensor(zi, zi, t2, ALU.subtract))
                for i, t in enumerate(tiles):
                    m = mag[:, t:t + 1].to_broadcast([P, T])
                    eng.tensor_tensor_scan(zr[:, i, :], m, zr[:, i, :], 0.0, ALU.mult, ALU.add)
                    ins = eng.tensor_tensor_scan(zi[:, i, :], m, zi[:, i, :], 0.0, ALU.mult, ALU.add)
                link(ins)
                if b >= 2:
                    eng.wait_ge(c_done, b - 1)
                eng.tensor_tensor(xs_re[0][:, b % 2], zr, c, ALU.mult)
                eng.scalar_tensor_tensor(xs_re[1][:, b % 2], zi, -1.0, s, ALU.mult, ALU.mult)
                eng.tensor_tensor(xs_im[0][:, b % 2], zr, s, ALU.mult)
                eng.tensor_tensor(xs_im[1][:, b % 2], zi, c, ALU.mult).then_inc(xs_ready, 1)
                eng.wait_ge(xs_ready, b + 1)
                if b == 1:
                    norm_v()
                    gating()
                if b % 4 == 0 and b:
                    combine(b // 4 - 1)
                if b:
                    take_columns(4 + b - 1)
            combine(QUADS - 1)
            take_columns(19)
            make_gain(1)
            make_gain(2).then_inc(mod_ready, 1)
            eng.wait_ge(glu_ready, 2)
            for i in range(2):
                eng.wait_ge(sig_ready, i + 1)
                eng.tensor_tensor(ab[:, 4 + 2 * i:6 + 2 * i, :], ab[:, 4 + 2 * i:6 + 2 * i, :], ub[:, 2 * i:2 * i + 2, :],
                                  ALU.mult).then_inc(ab_ready, 1)
            def low_parts(f):
                for n in range(3):
                    w = ffn_piece(f, n)[1]
                    eng.wait_ge(whi_ready, 3 * f + n + 1)
                    eng.tensor_tensor(ffn_piece(f, n, ring_r)[1], w, hi_piece(f, n).bitcast(F32), ALU.subtract).then_inc(wlo_ready, 1)

            residual(16, 4, proj_ready, lambda m: m + 1, 0, 4)
            take_columns(20)
            low_parts(0)
            low_parts(1)
            residual(16, 4, proj_ready, lambda m: m + 1, 4, KD)
            take_columns(21)
            norm(1)
            for i in range(2):
                eng.wait_ge(hhi_ready, i + 1)
                k = slice(4 * i, 4 * i + 4)
                eng.tensor_tensor(h_lo[:, k, :], h[:, k, :], h_hi[:, k, :].bitcast(F32), ALU.subtract)\
                    .then_inc(hlo_ready, 1)
            take_columns(22)
            take_columns(23)
            make_gain(3).then_inc(mod_ready, 1)
            low_parts(2)
            for f in range(F_DENSE):
                eng.wait_ge(silu_ready, f + 1)
                if f >= 4:
                    eng.wait_ge(down_done, f - 3)
                eng.tensor_tensor(act_hi[:, f % 4, :], silu_f[:, f % 4, :], bank[f % 4][:, T:2 * T], ALU.mult)
                link(eng.tensor_tensor(act_f[:, f % 4, :], silu_f[:, f % 4, :], bank[f % 4][:, T:2 * T], ALU.mult))
                eng.tensor_tensor(act_lo[:, f % 4, :], act_f[:, f % 4, :], act_hi[:, f % 4, :].bitcast(F32), ALU.subtract)\
                    .then_inc(actf_ready, 1)
                if f + 3 < F_DENSE:
                    low_parts(f + 3)
            residual(40, 4, down_done, lambda m: F_DENSE)
            norm(2)
            eng.wait_ge(pc_s, 16)
            eng.wait_ge(zss_ready, 1)
            eng.tensor_scalar(var2[:, 0, :], bank[4][:, 0:T], 1.0 / (QT * P), EPS, ALU.mult, ALU.add)
            link(eng.tensor_scalar(var2[:, 1, :], bank[4][:, T:2 * T], 1.0 / (KVT * P), EPS, ALU.mult, ALU.add))
            eng.reciprocal(var2, var2).then_inc(zvar_ready, 1)
            eng.wait_ge(rk_done, 1)
            eng.tensor_tensor(rope_tmp[:, 0, :], z[:, 5, :], cos_t, ALU.mult)
            link(eng.tensor_tensor(rope_tmp[:, 1, :], bank[5][:, 0:T], sin_t, ALU.mult))
            link(eng.tensor_tensor(k_rope, rope_tmp[:, 0, :], rope_tmp[:, 1, :], ALU.add))
            eng.wait_ge(zstd_ready, 1)
            for k in range(QT + KVT):
                g = kp("g_q")[:, k:k + 1] if k < QT else kp("g_kv")[:, k - QT:k - QT + 1]
                ins = eng.scalar_tensor_tensor(z[:, k, :], z[:, k, :], g, rstd2[:, int(k >= QT), :], ALU.mult, ALU.mult)
            ins.then_inc(lat_ready, 1)
            for job in range(1, 14, 2):
                eng.wait_ge(qk_mm, job + 1)
                eng.tensor_copy(job_out(job), bank[job % 4][:, :] if job >= 10 else
                                bank[job % 4][:, :].rearrange("p (a b) -> p a b", a=2)).then_inc(qk_dve, 1)
            eng.wait_ge(rq_done, 1)
            for i in range(2):
                c2 = cos_t.unsqueeze(1).to_broadcast([P, 2, T])
                s2 = sin_t.unsqueeze(1).to_broadcast([P, 2, T])
                link(eng.tensor_tensor(rope_tmp[:, 0:2, :], qr[:, 2 * i:2 * i + 2, :], c2, ALU.mult))
                link(eng.tensor_tensor(rope_tmp[:, 2:4, :], bank[4 + i][:, :].rearrange("p (a b) -> p a b", a=2), s2, ALU.mult))
                link(eng.tensor_tensor(qr[:, 2 * i:2 * i + 2, :], rope_tmp[:, 0:2, :], rope_tmp[:, 2:4, :], ALU.add))
            eng.sem_inc(rope_ready, 1)
            for hd in range(HEADS + 2):
                if hd < HEADS:
                    eng.wait_ge(score_ready, hd + 1)
                    if hd >= 2:
                        eng.wait_ge(exp_ready, hd - 1)
                    link(eng.tensor_reduce(rmax[:, hd % 2, :], bank[hd % 2][:, :].rearrange("p (a b) -> p a b", a=2),
                                           AX.X, ALU.max))
                    eng.tensor_scalar(rmax[:, hd % 2, :], rmax[:, hd % 2, :], -SCALE, None, ALU.mult).then_inc(max_ready, 1)
                    eng.wait_ge(exp_ready, hd + 1)
                    link(eng.reciprocal(rinv[:, hd % 2, :], rsum[:, hd % 2, :]))
                    for i in range(TT):
                        ins = eng.tensor_scalar(probs[:, hd % 2, i, :], probs[:, hd % 2, i, :], rinv[:, hd % 2, i:i + 1],
                                                None, ALU.mult)
                    ins.then_inc(probs_ready, 1)
                if hd >= 2:
                    g = hd - 2
                    eng.wait_ge(o_mm, g + 1)
                    eng.tensor_copy(att[:, g, :], bank[4 + g % 2][:, 0:T]).then_inc(o_ready, 1)
            residual(64, 0, proj_ready, lambda m: KD + m + 1)
            norm(3)
            eng.wait_ge(pd_s, 16)
            eng.wait_ge(logit_mm, 1)
            b3 = [P, TT, E_N]
            down = kp("down").unsqueeze(1).to_broadcast(b3)

            def wide(v):
                return v.unsqueeze(2).to_broadcast(b3)

            link(eng.tensor_copy(logit, bank[4][:, 0:16].rearrange("p (a b) -> p a b", a=TT)))

            def best(src, m, first):
                link(eng.tensor_reduce(top[:, m, :], src, AX.X, ALU.max))
                link(eng.tensor_tensor(is1, src, wide(top[:, m, :]), ALU.is_equal))
                link(eng.tensor_tensor(key, is1, down, ALU.mult))
                link(eng.tensor_reduce(top[:, m + 1, :], key, AX.X, ALU.max))
                link(eng.tensor_tensor(first, key, wide(top[:, m + 1, :]), ALU.is_equal))

            best(logit, 0, one1)
            link(eng.scalar_tensor_tensor(rest, one1, -3.0e38, logit, ALU.mult, ALU.add))
            best(rest, 2, one2)
            eng.tensor_tensor(taken, one1, one2, ALU.add).then_inc(taken_ready, 1)
            eng.tensor_tensor(gates[:, 0, :], top[:, 2, :], top[:, 0, :], ALU.subtract).then_inc(gdiff_ready, 1)
            eng.wait_ge(taken_ready, 1)
            eng.tensor_scalar(off_taken, taken, -OFF, OFF, ALU.mult, ALU.add)
            eng.memset(pos[:, :, E_N:E_N + 1], OFF)
            eng.memset(gate[:, :, E_N:E_N + 1], 0.0)
            eng.memset(plan[:, 1:SUBS + 1, 0:1], 0.0)
            eng.memset(plan[:, 0, :], 1.0)
            eng.wait_ge(pos_mm, 1)
            link(eng.tensor_copy(cnt, bank[5][:, 16:24]))
            link(eng.tensor_tensor(pos[:, :, 0:E_N], bank[5][:, 0:16].rearrange("p (a b) -> p a b", a=TT), off_taken, ALU.add))

            def pick_of(e):
                def body(s, n):
                    for i in range(TT):
                        ins = eng.tensor_scalar(pick[:, s, i, :], slot_no[:, s * P:s * P + SUB],
                                                pos[:, i, bass.ds(e, 1)], None, ALU.is_equal)
                    ins.then_inc(pick_ready[s], 1)

                return body

            pick_of(0)(0, 0)

            for sub in range(1, SUBS):
                link(eng.tensor_scalar(over, cnt, float(SUB * sub), None, ALU.is_gt))
                link(eng.tensor_tensor(plan[:, 0, 0:E_N], plan[:, 0, 0:E_N], over, ALU.add))
                link(eng.tensor_tensor_scan(plan[:, sub, 1:E_N + 1], kp("step"), over, 0.0, ALU.mult, ALU.add))
            link(eng.tensor_tensor_scan(plan[:, SUBS, 1:E_N + 1], kp("step"), plan[:, 0, 0:E_N], 0.0, ALU.mult, ALU.add))
            eng.tensor_copy(plan_int[0:1, :, :], plan[0:1, :, :]).then_inc(plan_ready, 1)
            eng.wait_ge(plan_ready, 1)
            for_subs(eng, plan_of(eng, 0), pick_of(0), later_only=True)
            eng.wait_ge(gexp_ready, 1)
            link(eng.tensor_scalar(gates[:, 2, :], gates[:, 1, :], 1.0, None, ALU.add))
            link(eng.reciprocal(gates[:, 3, :], gates[:, 2, :]))
            link(eng.tensor_tensor(gates[:, 4, :], gates[:, 3, :], gates[:, 1, :], ALU.mult))
            eng.tensor_tensor(gate_a, one1, wide(gates[:, 3, :]), ALU.mult)
            link(eng.tensor_tensor(gate_b, one2, wide(gates[:, 4, :]), ALU.mult))
            link(eng.tensor_tensor(gate[:, :, 0:E_N], gate_a, gate_b, ALU.add))
            with eng.Fori(0, E_N) as b:
                now, then = plan_of(eng, b), plan_of(eng, b + 1)

                def gated_pick(s, n):
                    for i in range(TT):
                        ins = eng.tensor_scalar(g_pick[:, s, i, :], slot_no[:, s * P:(s + 1) * P], pos[:, i, bass.ds(b, 1)],
                                                gate[:, i, bass.ds(b, 1)], ALU.is_equal, ALU.mult)
                    ins.then_inc(g_ready[s], 1)

                def product(s, n, c):
                    eng.wait_ge(e_silu[s], n * F_CHUNKS + c + 1)
                    eng.tensor_tensor(act_e[:, s, :], silu_e[:, s, :], bank[u_bank(c, s)][:, 256:512], ALU.mult)\
                        .then_inc(e_act[s], 1)

                for_subs(eng, now, gated_pick)
                for c in range(F_CHUNKS):
                    for_subs(eng, now, lambda s, n: product(s, n, c))
                for_subs(eng, then, pick_of(b + 1))

                def sum_out(s, n):
                    eng.wait_ge(e_down[s], n + 1)
                    eng.tensor_copy(ye[:, s, :], bank[SUM_BANK + s]).then_inc(ye_ready[s], 1)

                def add_back(s, n):
                    eng.wait_ge(y_added, (earlier + s) * 4 + 1)
                    for i in range(4):
                        eng.wait_ge(back_mm[s], n * 4 + i + 1)
                        two = y_moe.rearrange("p (a b) c -> p b a c", a=2)[:, i]
                        eng.tensor_tensor(two, two, bank[BACK_BANK[i]].rearrange("p (a b) -> p a b", a=2), ALU.add)\
                            .then_inc(y_added, 1)

                for_subs(eng, now, sum_out)
                earlier = eng.value_load(plan_int[0:1, SUBS, bass.ds(b, 1)], min_val=0, max_val=E_N * SUBS)
                for_subs(eng, now, add_back)
            earlier = eng.value_load(plan_int[0:1, SUBS, E_N:E_N + 1], min_val=E_N, max_val=E_N * SUBS)
            eng.wait_ge(y_added, earlier * 4 + 1)
            for m in range(KD):
                eng.scalar_tensor_tensor(x[:, m, :], y_moe[:, m, :], mod[:, 88 + m:89 + m], x[:, m, :],
                                         ALU.mult, ALU.add).then_inc(x_updated, 1)
            norm(4, True)

        @block.tensor
        def _(eng):
            def item(i, k):
                eng.wait_ge(item_in[i % SLOTS], 16 * (i // SLOTS + 1))
                n = SIZES[i]
                return ring[:, i % SLOTS, 0:n].rearrange("p (k n) -> p k n", k=k)

            def norm_sum(n):
                for k in range(KD):
                    if k % 2 == 0:
                        eng.wait_ge(sq_ready, KD // 2 * n + k // 2 + 1)
                    ins = eng.matmul(bank[SS_BANK[n]][:, 0:T], ones[:, :], sq[:, k, :], start=k == 0, stop=k == KD - 1)
                ins.then_inc(ss_ready, 1)

            def ada(a):
                w = item(I_ADA[a], KD)
                if a >= 2:
                    eng.wait_ge(col_used, a - 1)
                for k in range(KD):
                    for j in range(4):
                        ins = eng.matmul(bank[a % 2][32 * j:32 * j + 32, 0:P], cs_rows[:, k, :], w[:, k, j * P:(j + 1) * P],
                                         start=k == 0, stop=k == KD - 1, tile_position=(0, 32 * j))
                ins.then_inc(row_ready, 1)
                eng.wait_ge(row_ready, a + 1)
                eng.sem_inc(items_used, 1)

            def ada_turn(a):
                eng.wait_ge(row_copied, a + 1)
                eng.transpose(bank[a % 2][:, P:2 * P], row[:, a % 2, :], ident).then_inc(col_ready, 1)

            def h_ready(n, k=KD):
                if k % 4 == 0:
                    half = 2 if k >= 4 else 1
                    eng.wait_ge(h_act, 2 * n + half)
                    eng.wait_ge(h_dve, 2 * n + half)

            eng.wait_ge(ones_ready, 1)
            norm_sum(0)
            eng.wait_ge(cs_ready, 1)
            for a in range(4):
                ada(a)
                if a:
                    ada_turn(a - 1)
            ada_turn(3)

            def tiles4(i, base, ready):
                w = item(i, KD)
                for m in range(4):
                    for k in range(KD):
                        if i == I_B and m == 0:
                            h_ready(0, k)
                        ins = eng.matmul(bank[base + m // 2][:, (m % 2) * T:(m % 2) * T + T], w[:, k, m * P:(m + 1) * P],
                                         h[:, k, :], start=k == 0, stop=k == KD - 1)
                    if m == 3:
                        ins.then_inc(items_used, 1)
                        eng.wait_ge(items_used, i + 1)
                        eng.sem_inc(ready, 1)
                    elif m == 1:
                        ins.then_inc(ready, 1)

            def b_products(b):
                q, dr, jp = b // 4, (b // 2) % 2, b % 2
                if b == 0:
                    eng.wait_ge(uvb_act, 2)
                elif b >= 2:
                    eng.wait_ge(vw_used, b - 1)
                n = b // 2
                if jp == 0:
                    eng.wait_ge(b_loaded[n % 2], 16 * (n // 2 + 1))
                if dr:
                    eng.wait_ge(rev_ready, 1)
                src = ub_rev if dr else ub
                for i in range(2):
                    for o in range(2):
                        ins = eng.matmul(bank[2 + 2 * (b % 2) + i][:, o * T:(o + 1) * T],
                                         b_mat[:, n % 2, 2 * (2 * jp + i) + o, :], src[:, q, :], start=True, stop=True)
                ins.then_inc(vw_ready, 1)

            def c_products(b):
                q, dr, jp = b // 4, (b // 2) % 2, b % 2
                eng.wait_ge(xs_ready, b + 1)
                if q >= 2 and b % 4 == 0:
                    eng.wait_ge(yq_ready, q - 1)
                for n, (mat, xs) in enumerate(((c_re, xs_re[0]), (c_re, xs_re[1]), (c_im, xs_im[0]), (c_im, xs_im[1]))):
                    for i in range(2):
                        r, t = 32 * (2 * jp + i), dr * 16 + q * 4 + 2 * jp + i
                        ins = eng.matmul(bank[6 + q % 2][r:r + 32, dr * T:(dr + 1) * T], mat[:, t, :], xs[:, b % 2, i, :],
                                         start=n == 0, stop=n == 3, tile_position=(0, r))
                ins.then_inc(c_done, 1)

            tiles4(I_B, 6, uvb_ready)
            b_products(0)
            b_products(1)
            tiles4(I_U, 6, uvb_ready)
            w = item(I_V, KD)
            for i in range(TT):
                eng.wait_ge(uvb_act, 3 + i)
                for k in range(KD):
                    ins = eng.matmul(bank[6 + i], h[:, k, i * P:(i + 1) * P], w[:, k, :], start=k == 0, stop=k == KD - 1)
                ins.then_inc(uvb_ready, 1)
            eng.wait_ge(uvb_ready, 6)
            eng.sem_inc(items_used, 1)
            for b in range(BATCHES):
                ada(4 + b)
                if b:
                    ada_turn(4 + b - 1)
                if b == 0:
                    eng.wait_ge(v_ready, 1)
                    for g in range(HEADS_A):
                        for i in range(TT):
                            o = (g % 2) * T + i * P
                            ins = eng.matmul(bank[6 + g // 2][:, o:o + P], va[:, i, g * P:(g + 1) * P], w_s[:, g, :],
                                             start=True, stop=True)
                        if g % 2:
                            ins.then_inc(s_ready, 1)
                    eng.wait_ge(s_used, 1)
                    eng.wait_ge(cmat_ready, 1)
                c_products(b)
                if b + 2 < BATCHES:
                    b_products(b + 2)
            ada_turn(19)
            eng.wait_ge(gelu_ready, 1)
            w = item(I_GLU, 4)
            for m in range(4):
                for k in range(4):
                    ins = eng.matmul(bank[2 + m // 2][:, (m % 2) * T:(m % 2) * T + T], w[:, k, m * P:(m + 1) * P],
                                     ab[:, 4 + k, :], start=k == 0, stop=k == 3)
                if m % 2:
                    ins.then_inc(glu_ready, 1)
            eng.wait_ge(glu_ready, 2)
            eng.sem_inc(items_used, 1)

            def project(items, src, base, count, before=()):
                for i in range(2):
                    if before:
                        before[i]()
                    w = item(items[i], KD)
                    for m in range(4):
                        t = 4 * i + m
                        for k in range(KD):
                            ins = eng.matmul(bank[base + t // 2][:, (t % 2) * T:(t % 2) * T + T], w[:, k, m * P:(m + 1) * P],
                                             src[:, k, :], start=k == 0, stop=k == KD - 1)
                        if t % 2:
                            ins.then_inc(proj_ready, 2)
                    eng.wait_ge(proj_ready, count + 4 * i + 4)
                    eng.sem_inc(items_used, 1)

            eng.wait_ge(ab_ready, 2)
            def next_ada():
                ada_turn(20)
                ada(21)

            project(I_OUT, ab, 4, 0, (lambda: ada(20), next_ada))
            ada_turn(21)
            norm_sum(1)
            ada(22)
            ada(23)
            ada_turn(22)
            ada_turn(23)
            def up(f):
                c, r = f // 4, f % 4
                n = min(4, F_DENSE - 4 * c)
                eng.wait_ge(wlo_ready, 3 * f + 2)
                if f >= 4:
                    eng.wait_ge(actf_ready, f - 3)
                elif f < 2:
                    eng.wait_ge(col_used, 23 + f)
                for o, which in ((0, 0), (T, 1)):
                    high, low = hi_piece(f, which), ffn_piece(f, which, ring_r)[1]
                    for k in range(KD):
                        if f == 0 and which == 0 and k % 4 == 0:
                            eng.wait_ge(hlo_ready, k // 4 + 1)
                        for j, (w, v) in enumerate(((high, h_hi), (high, h_lo), (low, h_hi))):
                            ins = eng.matmul(bank[f % 4][:, o:o + T], w[:, k, :], v[:, k, :],
                                             start=k == 0 and j == 0, stop=k == KD - 1 and j == 2)
                ins.then_inc(up_ready, 1)
                if r == n - 1:
                    eng.wait_ge(up_ready, f + 1)
                    eng.sem_inc(items_used, 2)

            def down(f):
                c, r = f // 4, f % 4
                n = min(4, F_DENSE - 4 * c)
                eng.wait_ge(wlo_ready, 3 * f + 3)
                high, low = hi_piece(f, 2), ffn_piece(f, 2, ring_r)[1]
                eng.wait_ge(actf_ready, f + 1)
                for m in range(KD):
                    for j, (w, v) in enumerate(((high, act_hi), (high, act_lo), (low, act_hi))):
                        ins = eng.matmul(bank[4 + m // 2][:, (m % 2) * T:(m % 2) * T + T], w[:, m * P:(m + 1) * P],
                                         v[:, f % 4, :], start=f == 0 and m % 2 == 0 and j == 0,
                                         stop=f == F_DENSE - 1 and j == 2, skip_group_check=True)
                ins.then_inc(down_done, 1)
                if r == n - 1:
                    eng.wait_ge(down_done, f + 1)
                    eng.sem_inc(items_used, 1)

            up(0)
            up(1)
            for f in range(F_DENSE):
                down(f)
                if f + 2 < F_DENSE:
                    up(f + 2)
            norm_sum(2)
            wa, wb = item(I_MLA, KD), item(I_MLA + 1, KD)
            for m in range(6):
                w = wa[:, :, m * P:(m + 1) * P] if m < 4 else wb[:, :, (m - 4) * P:(m - 3) * P]
                for k in range(KD):
                    if m == 0:
                        h_ready(2, k)
                    ins = eng.matmul(bank[1 + m // 2][:, (m % 2) * T:(m % 2) * T + T], w[:, k, :], h[:, k, :],
                                     start=k == 0, stop=k == KD - 1)
                if m % 2:
                    ins.then_inc(z_ready, 1)
            eng.wait_ge(z_ready, 3)
            eng.sem_inc(items_used, 2)
            eng.wait_ge(zsq_ready, 1)
            for k in range(QT):
                eng.matmul(bank[4][:, 0:T], ones[:, :], sq[:, k, :], start=k == 0, stop=k == QT - 1)
            for k in range(KVT):
                ins = eng.matmul(bank[4][:, T:2 * T], ones[:, :], sq[:, QT + k, :], start=k == 0, stop=k == KVT - 1)
            ins.then_inc(zss_ready, 1)
            eng.wait_ge(pc_s, 16)
            eng.matmul(bank[5][:, 0:T], rot, z[:, 5, :], start=True, stop=True).then_inc(rk_done, 1)
            eng.wait_ge(lat_ready, 1)

            def job_begin(job):
                if job >= 4:
                    if job % 2 == 0:
                        eng.wait_ge(qk_act, job // 2 - 1)
                    else:
                        eng.wait_ge(qk_dve, job // 2 - 1)

            def two_tiles(job, w, kt, src0, col):
                job_begin(job)
                for i in range(2):
                    for k in range(kt):
                        ins = eng.matmul(bank[job % 4][:, i * T:(i + 1) * T], w[:, k, col + i * P:col + (i + 1) * P],
                                         z[:, src0 + k, :], start=k == 0, stop=k == kt - 1)
                ins.then_inc(qk_mm, 1)

            w = item(I_MLA + 2, QT)
            for job in range(4):
                two_tiles(job, w, QT, 0, job * 2 * P)
            w = item(I_MLA + 3, QT)
            for job in range(4, 6):
                two_tiles(job, w, QT, 0, (job - 4) * 2 * P)
            eng.wait_ge(qk_mm, 6)
            eng.sem_inc(items_used, 2)
            w = item(I_MLA + 4, 4)
            for job in range(6, 10):
                two_tiles(job, w[:, 0:2, :], KVT, QT, (job - 6) * 2 * P)
            for job in range(10, 14):
                job_begin(job)
                i, hf = (job - 10) // 2, (job - 10) % 2
                for k in range(KVT):
                    ins = eng.matmul(bank[job % 4][:, :], z[:, QT + k, i * P:(i + 1) * P], w[:, 2 + k, hf * 512:hf * 512 + 512],
                                     start=k == 0, stop=k == KVT - 1)
                ins.then_inc(qk_mm, 1)
            eng.wait_ge(qk_mm, 14)
            eng.sem_inc(items_used, 1)
            for i in range(4):
                ins = eng.matmul(bank[4 + i // 2][:, (i % 2) * T:(i % 2) * T + T], rot, qr[:, i, :], start=True, stop=True)
            ins.then_inc(rq_done, 1)
            eng.wait_ge(rope_ready, 1)
            eng.wait_ge(qk_act, 7)
            eng.wait_ge(qk_dve, 7)

            def scores(hd):
                if hd >= 2:
                    eng.wait_ge(exp_ready, hd - 1)
                r = 64 * (hd % 2)
                for i in range(TT):
                    o = bank[hd % 2][:, i * T:(i + 1) * T]
                    eng.matmul(o, qn[:, hd, i * P:(i + 1) * P], kn[:, hd, :], start=True, stop=False)
                    ins = eng.matmul(o, qr[r:r + 64, hd // 2, i * P:(i + 1) * P], k_rope[r:r + 64, :], start=False, stop=True)
                ins.then_inc(score_ready, 1)

            def turn_probs(hd):
                eng.wait_ge(probs_ready, hd + 1)
                if hd >= 2:
                    eng.wait_ge(pt_ready, hd - 1)
                for kt in range(TT):
                    for i in range(TT):
                        ins = eng.transpose(bank[2 + hd % 2][:, kt * T + i * P:kt * T + (i + 1) * P],
                                            probs[:, hd % 2, i, kt * P:(kt + 1) * P], ident)
                ins.then_inc(pt_mm, 1)

            def values(hd):
                eng.wait_ge(pt_ready, hd + 1)
                if hd >= 2:
                    eng.wait_ge(o_ready, hd - 1)
                for kt in range(TT):
                    ins = eng.matmul(bank[4 + hd % 2][:, 0:T], vv[:, kt, hd * P:(hd + 1) * P], probs_t[:, hd % 2, kt, :],
                                     start=kt == 0, stop=kt == TT - 1)
                ins.then_inc(o_mm, 1)

            scores(0)
            for hd in range(HEADS):
                if hd + 1 < HEADS:
                    scores(hd + 1)
                turn_probs(hd)
                if hd:
                    values(hd - 1)
            values(HEADS - 1)
            eng.wait_ge(o_ready, HEADS)
            project(I_WO, att, 0, KD)
            norm_sum(3)
            eng.wait_ge(pd_s, 16)
            for i in range(TT):
                for k in range(KD):
                    if i == 0:
                        h_ready(3, k)
                    ins = eng.matmul(bank[4][:, i * 8:i * 8 + 8], h[:, k, i * P:(i + 1) * P], router[:, k, :],
                                     start=k == 0, stop=k == KD - 1)
            ins.then_inc(logit_mm, 1)
            for i in range(4):
                tt, hf = i // 2, i % 2
                for k in range(4):
                    ins = eng.transpose(bank[i][:, k * P:(k + 1) * P], h[:, hf * 4 + k, tt * P:(tt + 1) * P], ident)
                ins.then_inc(tok_mm, 1)
            eng.wait_ge(taken_ready, 1)
            eng.matmul(bank[5][:, 0:8], tri, taken[:, 0, :], start=True, stop=True)
            eng.matmul(bank[5][:, 8:16], ones[:, :], taken[:, 0, :], start=True, stop=False)
            eng.matmul(bank[5][:, 8:16], tri, taken[:, 1, :], start=False, stop=True)
            eng.matmul(bank[5][:, 16:24], ones[:, :], taken[:, 0, :], start=True, stop=False)
            eng.matmul(bank[5][:, 16:24], ones[:, :], taken[:, 1, :], start=False, stop=True).then_inc(pos_mm, 1)
            eng.wait_ge(tok_act, 4)

            def gather(s, n, of):
                eng.wait_ge(pick_ready[s], n + 1)
                if s:
                    eng.wait_ge(hg_ready[s - 1], of[1][s - 1] + 1)
                for k in range(KD):
                    for i in range(TT):
                        ins = eng.matmul(bank[GATHER_BANK][:, k * SUB:(k + 1) * SUB], h_tok[:, i, k * P:(k + 1) * P],
                                         pick[:, s, i, :], start=i == 0, stop=i == TT - 1)
                ins.then_inc(hg_mm[s], 1)

            gather(0, 0, None)
            eng.wait_ge(plan_ready, 1)
            first = plan_of(eng, 0)
            for_subs(eng, first, lambda s, n: gather(s, n, first), later_only=True)
            with eng.Fori(0, E_N) as b:
                now, then = plan_of(eng, b), plan_of(eng, b + 1)
                earlier = eng.value_load(plan_int[0:1, SUBS, bass.ds(b, 1)], min_val=0, max_val=E_N * SUBS)

                def e_item(m, k):
                    i = I_MOE + m
                    eng.wait_ge(item_in[i % SLOTS], b * (16 * MOE_ITEMS // SLOTS) + 16 * (i // SLOTS + 1))
                    return ring[:, i % SLOTS, :].rearrange("p (k n) -> p k n", k=k)

                def turn(s, n, c):
                    eng.wait_ge(e_act[s], n * F_CHUNKS + c + 1)
                    if s:
                        eng.wait_ge(e_copied[s - 1], now[1][s - 1] * F_CHUNKS + c + 1)
                    for q in range(2):
                        ins = eng.transpose(bank[TURN_BANK][:, q * P:(q + 1) * P], act_e[:, s, q * P:(q + 1) * P], ident)
                    ins.then_inc(e_turned[s], 1)

                def up(s, n, c, used):
                    if c == 0:
                        eng.wait_ge(hg_ready[s], n + 1)
                    if s >= 2:
                        before = 0 if s == 2 else 2
                        eng.wait_ge(e_act[before], now[1][before] * F_CHUNKS + c + 1)
                    if s == 1:
                        if c:
                            eng.wait_ge(e_act[s], n * F_CHUNKS + c)
                        else:
                            eng.wait_ge(y_added, earlier * 4 + 1)
                    for o, m in ((0, UP_ITEM[c]), (256, UP_ITEM[c] + 1)):
                        w = e_item(m, KD)
                        for k in range(KD):
                            for j in range(2):
                                ins = eng.matmul(bank[u_bank(c, s)][64 * j:64 * j + 64, o:o + 256], hg[:, s, k, :],
                                                 w[:, k, 256 * j:256 * j + 256], start=k == 0, stop=k == KD - 1,
                                                 tile_position=(0, 64 * j))
                                if s == 0 and used and o == 0 and k == 0 and j == 0:
                                    ins.then_inc(items_used, used)
                        if o == 0 and c:
                            turn(s, n, c - 1)
                    ins.then_inc(e_up[s], 1)

                def down(s, n, c, used):
                    w = e_item(DOWN_ITEM[c], 4)
                    eng.wait_ge(e_copied[s], n * F_CHUNKS + c + 1)
                    if c == 0:
                        eng.wait_ge(spread_ready[s], n + 1)
                    for t in range(4):
                        for j in range(2):
                            ins = eng.matmul(bank[SUM_BANK + s][64 * j:64 * j + 64, :],
                                             act_t[:, s, (t % 2) * P + (t // 2) * 64:(t % 2) * P + (t // 2) * 64 + 64],
                                             w[:, t, 512 * j:512 * j + 512], start=c == 0 and t == 0,
                                             stop=c == F_CHUNKS - 1 and t == 3, tile_position=(0, 64 * j))
                            if s == 0 and t == 0 and j == 0:
                                ins.then_inc(items_used, used)
                    if c == F_CHUNKS - 1:
                        ins.then_inc(e_down[s], 1)

                def spread_turn(s, n):
                    eng.wait_ge(g_ready[s], n + 1)
                    for i in range(TT):
                        ins = eng.transpose(bank[SUM_BANK + s][:, i * P:(i + 1) * P], g_pick[:, s, i, :], ident)
                    ins.then_inc(spread_mm[s], 1)

                def back(s, n):
                    eng.wait_ge(ye_ready[s], n + 1)
                    for i in range(4):
                        if s or i >= 2:
                            eng.wait_ge(y_added, (earlier + s) * 4 + i)
                        for j in range(2):
                            ins = eng.matmul(bank[BACK_BANK[i]][:, j * T:(j + 1) * T], ye[:, s, i * P:(i + 1) * P],
                                             spread[:, s, j * T:(j + 1) * T], start=True, stop=True)
                            if s == 0 and i == 0 and j == 0:
                                ins.then_inc(items_used, 1)
                        ins.then_inc(back_mm[s], 1)

                for_subs(eng, now, lambda s, n: up(s, n, 0, 0))
                for_subs(eng, now, spread_turn)
                eng.wait_ge(y_added, earlier * 4 + 1)
                for c in range(F_CHUNKS - 1):
                    for_subs(eng, now, lambda s, n: up(s, n, c + 1, 2 if c == 0 else 1))
                    for_subs(eng, now, lambda s, n: down(s, n, c, 2))
                for_subs(eng, now, lambda s, n: turn(s, n, F_CHUNKS - 1))
                for_subs(eng, then, lambda s, n: gather(s, n, then))
                for_subs(eng, now, lambda s, n: down(s, n, F_CHUNKS - 1, 1))
                for_subs(eng, now, back)
            norm_sum(4)


UP_ITEM, DOWN_ITEM, MOE_ORDER = [], [], []
for _c in range(F_CHUNKS + 1):
    if _c < F_CHUNKS:
        UP_ITEM.append(len(MOE_ORDER))
        MOE_ORDER += [("w1", _c), ("w3", _c)]
    if _c:
        DOWN_ITEM.append(len(MOE_ORDER))
        MOE_ORDER += [("w2", _c - 1)]


def layout(inp):
    import numpy as np

    f = np.float32
    a = {k: np.asarray(v) for k, v in inp.items()}

    def col(v):
        return np.asarray(v, f).reshape(-1, P).T

    def tiles(w, n):
        k = w.shape[0] // P
        return w.reshape(k, P, w.shape[1]).transpose(1, 0, 2).reshape(P, -1)

    out = {}
    out["x"] = np.ascontiguousarray(a["x"][0].T.reshape(KD, P, T).transpose(1, 0, 2))
    keep = np.zeros((P, N_KEEP), f)

    def put(dst, table, name, v):
        s, e = table[name]
        dst[:, s:e] = v

    put(keep, COLS, "c", col(a["c"][0]))
    put(keep, COLS, "ada_b", col(a["ada_b"].reshape(-1)))
    put(keep, COLS, "g_mix", col(a["norm_mix_g"].reshape(-1)))
    put(keep, COLS, "g_ffn", col(a["norm_ffn_g"].reshape(-1)))
    put(keep, COLS, "g_fin", col(a["final_g"]))
    put(keep, COLS, "g_sgu", a["sgu_v_g"][0].T)
    put(keep, COLS, "d_skip", col(a["s5_d"][0]))
    put(keep, COLS, "g_q", col(a["mla_q_norm_g"][0]))
    put(keep, COLS, "g_kv", col(a["mla_kv_norm_g"][0]))
    put(keep, COLS, "half_pi", np.pi / 2)
    put(keep, COLS, "ident", np.eye(P, dtype=f))
    put(keep, COLS, "step", 1.0)
    put(keep, COLS, "down", np.arange(E_N, 0, -1, dtype=f)[None, :])
    out["keep"] = keep

    pa = np.zeros((P, N_A), f)
    m = np.zeros((4, 2, 4, 2, 16, 4, 2, 2, STATE), f)
    for n, src in enumerate((a["s5_b_re"][0], a["s5_b_im"][0])):
        s = src.reshape(2, 4, 4, 2, STATE, 16)
        for pr in range(4):
            for g in range(2):
                m[:, :, pr, g, :, pr, n, g, :] = s[:, :, pr, g].transpose(1, 0, 3, 2)
    out["pb"] = m.reshape(8, P, 8, P)
    for name, src in (("c_re", a["s5_c_re"][0]), ("c_im", a["s5_c_im"][0])):
        m = np.zeros((2, STATE, S5_TILES, 2, 16), f)
        s = src.reshape(S5_TILES, 2, 16, STATE)
        for g in range(2):
            m[g, :, :, g, :] = s[:, g].transpose(2, 0, 1)
        put(pa, COLS_A, name, m.reshape(P, -1))
    put(pa, COLS_A, "lam_re", a["s5_lam_re"][0].reshape(S5_TILES, P).T)
    put(pa, COLS_A, "lam_im", a["s5_lam_im"][0].reshape(S5_TILES, P).T)
    put(pa, COLS_A, "log_dt", np.repeat(a["s5_log_dt"][0].reshape(S5_TILES, 2).T, STATE, axis=0))
    put(pa, COLS_A, "w_s", a["sgu_w_s"][0].transpose(2, 0, 1).reshape(P, -1))
    put(pa, COLS_A, "b_s", np.broadcast_to(a["sgu_b_s"][0].reshape(1, -1), (P, 512)))
    put(pa, COLS_A, "iota", np.arange(T, dtype=f)[None, :])
    out["pa"] = pa

    pc = np.zeros((P, N_C), f)
    inv = 10000.0 ** (-np.arange(0, 64, 2, dtype=f) / f(64))
    ang = np.arange(T, dtype=f)[None, :] * inv.astype(f)[:, None]
    put(pc, COLS_C, "cos", np.tile(np.cos(ang), (4, 1)))
    put(pc, COLS_C, "sin", np.tile(np.concatenate([-np.sin(ang), np.sin(ang)]), (2, 1)))
    rot = np.zeros((P, P), f)
    for r in range(P):
        rot[r ^ 32, r] = 1.0
    put(pc, COLS_C, "rot", rot)
    out["pc"] = pc

    pd = np.zeros((P, N_D), f)
    put(pd, COLS_D, "router", tiles(a["moe_w_router"][0], 8))
    put(pd, COLS_D, "slot", (np.arange(SUBS)[:, None] * SUB + np.arange(P)[None, :] % SUB).reshape(1, -1))
    put(pd, COLS_D, "tri", np.triu(np.ones((P, P), f), 1))
    out["pd"] = pd

    pre = np.zeros((I_MOE, P, ITEM), f)

    def item(i, w):
        pre[i, :, 0:w.shape[1]] = w

    for layer in range(2):
        for j in range(12):
            n = layer * 12 + j
            item(I_ADA[n], tiles(a["ada_w"][layer][:, j * 512:(j + 1) * 512], 512))
    for j, i in enumerate((I_U, I_V, I_B)):
        item(i, tiles(a["ab_w_in"][0][:, j * 512:(j + 1) * 512], 512))
    item(I_GLU, tiles(a["s5_w_glu"][0], 512))
    for j in range(2):
        item(I_OUT[j], tiles(a["ab_w_out"][0][:, j * 512:(j + 1) * 512], 512))
        item(I_WO[j], tiles(a["mla_w_o"][0][:, j * 512:(j + 1) * 512], 512))
    for j in range(6):
        cut = slice(j * 512, min((j + 1) * 512, F_DENSE * P))
        item(I_FFN + 3 * j, tiles(a["ffn_w1"][0][:, cut], 512))
        item(I_FFN + 3 * j + 1, tiles(a["ffn_w3"][0][:, cut], 512))
        item(I_FFN + 3 * j + 2, tiles(a["ffn_w2"][0][cut], D))
    w = a["mla_w_in"][0]
    item(I_MLA, tiles(w[:, 0:512], 512))
    item(I_MLA + 1, tiles(np.concatenate([w[:, 512:640], w[:, 640:704], w[:, 640:704]], axis=1), 256))
    uq = a["mla_w_uq"][0].reshape(-1, HEADS, 192)
    item(I_MLA + 2, tiles(uq[:, :, 0:128].reshape(-1, 1024), 1024))
    item(I_MLA + 3, tiles(uq[:, :, 128:192].reshape(-1, 512), 512))
    ukv = a["mla_w_ukv"][0].reshape(-1, HEADS, 256)
    item(I_MLA + 4, np.concatenate([tiles(ukv[:, :, 0:128].reshape(-1, 1024), 1024),
                                    tiles(ukv[:, :, 128:256].reshape(-1, 1024), 1024)], axis=1))
    out["pre"] = pre

    moe = np.zeros((E_N, MOE_ITEMS, P, ITEM), f)
    for n, (which, c) in enumerate(MOE_ORDER):
        w = a["moe_" + which][0]
        if which == "w2":
            moe[:, n] = w[:, c * 512:(c + 1) * 512].reshape(E_N, 4, P, D).transpose(0, 2, 1, 3).reshape(E_N, P, ITEM)
        else:
            moe[:, n] = w[:, :, c * 512:(c + 1) * 512].reshape(E_N, KD, P, 512).transpose(0, 2, 1, 3).reshape(E_N, P, ITEM)
    out["moe"] = moe
    return out


def program(nc, shapes):
    args = [nc.dram_tensor(f"in_{n}", s, F32, kind="ExternalInput").ap() for n, s in shapes.items()]
    out = nc.dram_tensor("out_0", (P, KD, T), F32, kind="ExternalOutput").ap()
    trunk(nc, *args, out)


def kernel(**inputs):
    import numpy as np
    import concourse.bacc as bacc
    from concourse.bass_utils import run_bass_kernel_spmd

    arrays = layout(inputs)
    nc = bacc.Bacc("TRN2", target_bir_lowering=False, num_devices=1)
    program(nc, {n: arrays[n].shape for n in ("x", "keep", "pa", "pb", "pc", "pd", "pre", "moe")})
    r = run_bass_kernel_spmd(nc, [{f"in_{n}": v for n, v in arrays.items()}], core_ids=[0])
    y = np.asarray(r.results[0]["out_0"])
    return np.ascontiguousarray(y.transpose(1, 0, 2).reshape(D, T).T).reshape(1, T, D)
```
